# Optimizing a Trainium2 kernel written in Bass

```python
import math
import jax, jax.numpy as jnp
from jax import lax
import numpy as np

D_MODEL = 1024
BATCH = 1
SEQ = 512
DEPTH = 2

HEAD_DIM = 64
N_MIXERS = 4
N_HEADS_TOTAL = D_MODEL // HEAD_DIM
G = N_HEADS_TOTAL // N_MIXERS
HW = G * HEAD_DIM
MIX_WIDTH = N_MIXERS * HW
Q_BLOCK = 128
MOBA_BLOCK = 256
MOBA_TOPK = 3
MOBA_QCHUNK = 64
MLA_Q_RANK = D_MODEL // 4
MLA_KV_RANK = D_MODEL // 8
MLA_NOPE_DIM = HEAD_DIM
MLA_ROPE_DIM = HEAD_DIM // 2
MLA_V_DIM = HEAD_DIM
ROPE_THETA = 10000.0
DIL_PAIRS = ((128, 1), (512, 4), (2048, 16))
N_ALIBI_HEADS = 2 * G
D_FF = 256 * (-(-(8 * D_MODEL) // (3 * 256)))
RMS_EPS = 1e-6
NEG_INF = -1e30
MIX_SPLIT_WIDTHS = (HW, HW, HW, HW, HW, HW, G, MLA_Q_RANK, MLA_KV_RANK, MLA_ROPE_DIM, HW, HW, HW)
IN_WIDTH = sum(MIX_SPLIT_WIDTHS)
SPLIT_POINTS = tuple(int(v) for v in np.cumsum(MIX_SPLIT_WIDTHS)[:-1])

kernel_name = 'hymba_style_moba_fox_mla_dilated_macaron'

def _rmsnorm(x, g):
    xf = x.astype(jnp.float32)
    y = xf * lax.rsqrt(jnp.mean(xf * xf, axis=-1, keepdims=True) + RMS_EPS)
    return (y * g.astype(jnp.float32)).astype(x.dtype)

def _swiglu(h, w_gate, w_up, w_down):
    return (jax.nn.silu(h @ w_gate) * (h @ w_up)) @ w_down

def _to_heads(a):
    B, T, _ = a.shape
    return a.reshape(B, T, G, -1).transpose(0, 2, 1, 3)

def _from_heads(a):
    B, H, T, d = a.shape
    return a.transpose(0, 2, 1, 3).reshape(B, T, H * d)

def _alibi_slopes():
    s = np.array([2.0 ** (-8.0 * (i + 1) / N_ALIBI_HEADS) for i in range(N_ALIBI_HEADS)], dtype=np.float32)
    return jnp.asarray(s[1::2]), jnp.asarray(s[0::2])

def _rope_tables(T):
    inv = ROPE_THETA ** (-jnp.arange(0, MLA_ROPE_DIM, 2, dtype=jnp.float32) / MLA_ROPE_DIM)
    ang = jnp.arange(T, dtype=jnp.float32)[:, None] * inv[None, :]
    return jnp.cos(ang), jnp.sin(ang)

def _rope(x, cos, sin):
    half = x.shape[-1] // 2
    x1, x2 = x[..., :half], x[..., half:]
    c = cos[None, :, None, :].astype(x.dtype)
    s = sin[None, :, None, :].astype(x.dtype)
    return jnp.concatenate([x1 * c - x2 * s, x1 * s + x2 * c], axis=-1)

def _causal_block_attention(q, k, v, decay=None):
    B, H, T, dq = q.shape
    scale = dq ** -0.5
    kpos = jnp.arange(T)

    def block(start):
        qb = lax.dynamic_slice_in_dim(q, start, Q_BLOCK, axis=2)
        t = start + jnp.arange(Q_BLOCK)
        s = jnp.einsum('bhqd,bhkd->bhqk', qb, k).astype(jnp.float32) * scale
        if decay is not None:
            s = s + lax.dynamic_slice_in_dim(decay, start, Q_BLOCK, axis=2)[..., None] - decay[:, :, None, :]
        s = jnp.where(kpos[None, :] <= t[:, None], s, NEG_INF)
        p = jax.nn.softmax(s, axis=-1).astype(v.dtype)
        return jnp.einsum('bhqk,bhkd->bhqd', p, v)

    out = lax.map(block, jnp.arange(T // Q_BLOCK) * Q_BLOCK)
    return jnp.moveaxis(out, 0, 2).reshape(B, H, T, v.shape[-1])

def _moba_attention(q, k, v, slopes):
    B, H, T, hd = q.shape
    blk = MOBA_BLOCK
    Tp = -(-T // blk) * blk
    pad = ((0, 0), (0, 0), (0, Tp - T), (0, 0))
    q, k, v = jnp.pad(q, pad), jnp.pad(k, pad), jnp.pad(v, pad)
    nb = Tp // blk
    kb = k.reshape(B, H, nb, blk, hd)
    vb = v.reshape(B, H, nb, blk, hd)
    kmean = jnp.mean(kb.astype(jnp.float32), axis=3)
    topk = min(MOBA_TOPK, nb)
    scale = hd ** -0.5
    bi = jnp.arange(B)[:, None, None, None]
    hi = jnp.arange(H)[None, :, None, None]
    blk_ids = jnp.arange(nb)
    offs = jnp.arange(blk)

    def chunk(start):
        qc = lax.dynamic_slice_in_dim(q, start, MOBA_QCHUNK, axis=2)
        t = start + jnp.arange(MOBA_QCHUNK)
        cur = start // blk
        gate = jnp.einsum('bhqd,bhnd->bhqn', qc.astype(jnp.float32), kmean)
        gate = jnp.where(blk_ids < cur, gate, NEG_INF)
        idx = lax.top_k(gate, topk)[1]
        k_sel = kb[bi, hi, idx]
        v_sel = vb[bi, hi, idx]
        dist_sel = t[:, None, None] - (idx[..., None] * blk + offs)
        s_sel = (jnp.einsum('bhqd,bhqjkd->bhqjk', qc, k_sel).astype(jnp.float32) * scale
                 - slopes[:, None, None, None] * dist_sel)
        s_sel = jnp.where((idx < cur)[..., None], s_sel, NEG_INF)
        k_own = lax.dynamic_slice_in_dim(k, cur * blk, blk, axis=2)
        v_own = lax.dynamic_slice_in_dim(v, cur * blk, blk, axis=2)
        dist_own = t[:, None] - (cur * blk + offs)[None, :]
        s_own = (jnp.einsum('bhqd,bhkd->bhqk', qc, k_own).astype(jnp.float32) * scale
                 - slopes[:, None, None] * dist_own)
        s_own = jnp.where(dist_own >= 0, s_own, NEG_INF)
        s = jnp.concatenate([s_sel.reshape(B, H, MOBA_QCHUNK, topk * blk), s_own], axis=-1)
        p = jax.nn.softmax(s, axis=-1).astype(v.dtype)
        p_sel = p[..., :topk * blk].reshape(B, H, MOBA_QCHUNK, topk, blk)
        p_own = p[..., topk * blk:]
        return (jnp.einsum('bhqjk,bhqjkd->bhqd', p_sel, v_sel)
                + jnp.einsum('bhqk,bhkd->bhqd', p_own, v_own))

    out = lax.map(chunk, jnp.arange(Tp // MOBA_QCHUNK) * MOBA_QCHUNK)
    return jnp.moveaxis(out, 0, 2).reshape(B, H, Tp, hd)[:, :, :T]

def _mla_attention(c_q, c_kv, k_rope, q_norm, kv_norm, w_uq, w_ukv, cos, sin):
    B, T, _ = c_q.shape
    q = (_rmsnorm(c_q, q_norm) @ w_uq).reshape(B, T, G, MLA_NOPE_DIM + MLA_ROPE_DIM)
    kv = (_rmsnorm(c_kv, kv_norm) @ w_ukv).reshape(B, T, G, MLA_NOPE_DIM + MLA_V_DIM)
    q_nope, q_rot = q[..., :MLA_NOPE_DIM], q[..., MLA_NOPE_DIM:]
    k_nope, v = kv[..., :MLA_NOPE_DIM], kv[..., MLA_NOPE_DIM:]
    q_rot = _rope(q_rot, cos, sin)
    k_rot = jnp.broadcast_to(_rope(k_rope[:, :, None, :], cos, sin), (B, T, G, MLA_ROPE_DIM))
    qh = jnp.concatenate([q_nope, q_rot], axis=-1).transpose(0, 2, 1, 3)
    kh = jnp.concatenate([k_nope, k_rot], axis=-1).transpose(0, 2, 1, 3)
    return _causal_block_attention(qh, kh, v.transpose(0, 2, 1, 3))

def _dilated_branch(q, k, v, slopes, window, dil):
    B, H, T, hd = q.shape
    span = window // dil
    L = T // dil
    nb = -(-L // span)
    Lp = nb * span

    def by_residue(a):
        a = a.reshape(B, H, L, dil, hd).transpose(0, 1, 3, 2, 4)
        a = jnp.pad(a, ((0, 0), (0, 0), (0, 0), (0, Lp - L), (0, 0)))
        return a.reshape(B, H, dil, nb, span, hd)

    def with_prev(a):
        prev = jnp.pad(a, ((0, 0), (0, 0), (0, 0), (1, 0), (0, 0), (0, 0)))[:, :, :, :-1]
        return jnp.concatenate([prev, a], axis=4)

    qb = by_residue(q)
    kb = with_prev(by_residue(k))
    vb = with_prev(by_residue(v))
    qi = jnp.arange(span)[:, None]
    kj = jnp.arange(2 * span)[None, :]
    delta = span + qi - kj
    key_idx = (jnp.arange(nb)[:, None, None] - 1) * span + kj[None]
    valid = (delta >= 0) & (delta <= span) & (key_idx >= 0)
    s = (jnp.einsum('bhrnqd,bhrnkd->bhrnqk', qb, kb).astype(jnp.float32) * hd ** -0.5
         - slopes[:, None, None, None, None] * (delta * dil).astype(jnp.float32))
    s = jnp.where(valid, s, NEG_INF)
    lse = jax.nn.logsumexp(s, axis=-1)
    p = jnp.exp(s - lse[..., None]).astype(v.dtype)
    o = jnp.einsum('bhrnqk,bhrnkd->bhrnqd', p, vb)
    o = o.reshape(B, H, dil, Lp, hd)[:, :, :, :L].transpose(0, 1, 3, 2, 4).reshape(B, H, T, hd)
    lse = lse.reshape(B, H, dil, Lp)[..., :L].transpose(0, 1, 3, 2).reshape(B, H, T)
    return o, lse

def _dilated_attention(q, k, v, slopes):
    branches = [_dilated_branch(q, k, v, slopes, w, d) for (w, d) in DIL_PAIRS]
    o = jnp.stack([b[0] for b in branches]).astype(jnp.float32)
    wts = jax.nn.softmax(jnp.stack([b[1] for b in branches]), axis=0)
    return jnp.sum(wts[..., None] * o, axis=0).astype(q.dtype)

def setup_inputs(seed: int = 0) -> dict:
    key = jax.random.key(seed)
    ks = jax.random.split(key, 18)
    f32 = jnp.float32
    L, D = DEPTH, D_MODEL

    def w(k, shape, fan_in):
        return jax.random.normal(k, shape, f32) * fan_in ** -0.5

    def gain(k, shape):
        return 1.0 + 0.1 * jax.random.normal(k, shape, f32)

    return {
        'x': jax.random.normal(ks[0], (BATCH, SEQ, D), f32),
        'norm_ffn1': gain(ks[1], (L, D)),
        'ffn1_gate': w(ks[2], (L, D, D_FF), D),
        'ffn1_up': w(ks[3], (L, D, D_FF), D),
        'ffn1_down': w(ks[4], (L, D_FF, D), D_FF),
        'norm_mix': gain(ks[5], (L, D)),
        'w_in': w(ks[6], (L, D, IN_WIDTH), D),
        'forget_bias': jax.random.uniform(ks[7], (L, G), f32, 1.0, 4.0),
        'mla_q_norm': gain(ks[8], (L, MLA_Q_RANK)),
        'mla_kv_norm': gain(ks[9], (L, MLA_KV_RANK)),
        'w_uq': w(ks[10], (L, MLA_Q_RANK, G * (MLA_NOPE_DIM + MLA_ROPE_DIM)), MLA_Q_RANK),
        'w_ukv': w(ks[11], (L, MLA_KV_RANK, G * (MLA_NOPE_DIM + MLA_V_DIM)), MLA_KV_RANK),
        'w_out': w(ks[12], (L, MIX_WIDTH, D), MIX_WIDTH),
        'norm_ffn2': gain(ks[13], (L, D)),
        'ffn2_gate': w(ks[14], (L, D, D_FF), D),
        'ffn2_up': w(ks[15], (L, D, D_FF), D),
        'ffn2_down': w(ks[16], (L, D_FF, D), D_FF),
        'norm_final': gain(ks[17], (D,)),
    }

def reference(x, norm_ffn1, ffn1_gate, ffn1_up, ffn1_down, norm_mix, w_in, forget_bias,
              mla_q_norm, mla_kv_norm, w_uq, w_ukv, w_out, norm_ffn2, ffn2_gate, ffn2_up,
              ffn2_down, norm_final):
    T = x.shape[1]
    slopes_moba, slopes_dil = _alibi_slopes()
    cos, sin = _rope_tables(T)
    for l in range(DEPTH):
        x = x + 0.5 * _swiglu(_rmsnorm(x, norm_ffn1[l]), ffn1_gate[l], ffn1_up[l], ffn1_down[l])
        h = _rmsnorm(x, norm_mix[l])
        (aq, ak, av, bq, bk, bv, bf, cq, ckv, ckr, dq, dk, dv) = jnp.split(h @ w_in[l], SPLIT_POINTS, axis=-1)
        o_a = _moba_attention(_to_heads(aq), _to_heads(ak), _to_heads(av), slopes_moba)
        logf = jax.nn.log_sigmoid((bf + forget_bias[l]).astype(jnp.float32)).transpose(0, 2, 1)
        o_b = _causal_block_attention(_to_heads(bq), _to_heads(bk), _to_heads(bv),
                                      decay=jnp.cumsum(logf, axis=-1))
        o_c = _mla_attention(cq, ckv, ckr, mla_q_norm[l], mla_kv_norm[l], w_uq[l], w_ukv[l], cos, sin)
        o_d = _dilated_attention(_to_heads(dq), _to_heads(dk), _to_heads(dv), slopes_dil)
        mixed = jnp.concatenate([_from_heads(o_a), _from_heads(o_b), _from_heads(o_c), _from_heads(o_d)], axis=-1)
        x = x + mixed @ w_out[l]
        x = x + 0.5 * _swiglu(_rmsnorm(x, norm_ffn2[l]), ffn2_gate[l], ffn2_up[l], ffn2_down[l])
    return _rmsnorm(x, norm_final)


_drawn_inputs = setup_inputs


def setup_inputs(seed=0):
    import zlib

    import numpy as np

    out = dict(_drawn_inputs(seed))
    spreads = {}
    factors = {'mla_q_norm': 5.824, 'mla_kv_norm': 3.174}
    for name, (base, spread) in spreads.items():
        noise = np.random.default_rng([zlib.crc32(name.encode()), seed]).standard_normal(out[name].shape)
        drawn = base * np.exp(spread * noise) if base else spread * noise
        out[name] = __import__('jax').numpy.asarray(drawn.astype(out[name].dtype))
    for name, factor in factors.items():
        out[name] = (out[name] * factor).astype(out[name].dtype)
    return out
```

```python
from contextlib import ExitStack

import numpy as np

import concourse.bass as bass
from concourse import mybir

F32 = mybir.dt.float32
F32R = mybir.dt.float32r
ALU = mybir.AluOpType
ACT = mybir.ActivationFunctionType

P = 128
D = 1024
T = 512
DEPTH = 2
KD = D // P
QT = T // P
HD = 64
G = 4
HW = G * HD
FF = 256 * (-(-(8 * D) // (3 * 256)))
KF = FF // P
Q_RANK, KV_RANK, ROPE = D // 4, D // 8, HD // 2
EPS = 1e-6
NEG = -1e30
BIG = 3e38
SCALE = HD ** -0.5
SCALE_MLA = (HD + ROPE) ** -0.5

AQ, AK, AV, BQ, BK, BV = (HW * i for i in range(6))
BF = 6 * HW
CQ = BF + G
CKV = CQ + Q_RANK
CKR = CKV + KV_RANK
DQ = CKR + ROPE
DK, DV = DQ + HW, DQ + 2 * HW

BLK = 256
GU_STEPS = FF // BLK
DN_K = (8, 8, KF - 16)
DN_PAIRS = D // BLK
DN_STEPS = 3 * DN_PAIRS // 2
FFN_STEPS = GU_STEPS + DN_STEPS
MIX_STEPS = 8
LAYER_STEPS = 2 * FFN_STEPS + MIX_STEPS
MIX0, FFN2 = FFN_STEPS, FFN_STEPS + MIX_STEPS

MIX_HEAD_OUTS = 14
MIX_OUTS = 30

U_FFN1, U_MIX, U_LQ, U_LKV = 0, 1, 2, 3
U_VT = {"C": 4, "A": 6, "B": 10, "D": 14}
U_OT = {"C": 8, "A": 12, "B": 16, "D": 18}
U_FFN2 = 20
LAYER_USES = 21
NORMS = 5
N_FFN1, N_MIX, N_LQ, N_LKV, N_FFN2 = range(NORMS)
LAYER_X = 3 * KD

ORDER = "CABD"
ROWS = {"A": 0, "B": 2, "C": 4, "D": 6}
HEADS = 4 * G

SCORED = {0: (2, 1), 1: (2, 2), 2: (2, 3), 4: (3, 1), 5: (3, 2), 6: (3, 3), 7: (4, 0), 8: (4, 1), 9: (4, 3),
          10: (5, 0), 11: (5, 2), 12: (5, 3)}
LATER = {3: (3, 0), 8: (4, 2), 10: (5, 1)}
SLOT_VT = {0: "C", 3: "A", 9: "B", 13: "D"}
SLOT_OT = {6: "C", 10: "A", 14: "B"}
DEST = {(1, 0): "qA0", (1, 1): "qA1", (2, 0): "kA0", (2, 1): "kA1", (2, 2): "vA0", (2, 3): "vA1",
        (3, 0): "qB0", (3, 1): "qB1", (3, 2): "kB0", (3, 3): "kB1", (4, 0): "vB0", (4, 1): "vB1",
        (4, 2): "qD0", (4, 3): "qD1", (5, 0): "kD0", (5, 1): "kD1", (5, 2): "vD0", (5, 3): "vD1"}
MIX_COLS = {(1, 0): AQ, (2, 0): AK, (2, 1): AV, (3, 0): BQ, (3, 1): BK, (4, 0): BV, (4, 1): DQ,
            (5, 0): DK, (5, 1): DV}

TRI = [P * i * (i + 1) // 2 for i in range(QT + 1)]
TRT = [0, T, 2 * T, 2 * T - P]


def mix_out(s, p, o=0):
    base = {0: 0, 1: 4}.get(s, 14 + 4 * (s - 2))
    if s == 1:
        return base + {0: 0, 1: 1, 2: 2, 3: 6}[p] + o
    return base + p


def out_bank(j):
    return (j % 4, j - 4) if j < MIX_HEAD_OUTS else (j % 2, j - 2)


def freed_panels(n):
    return [slots[m] for slots, m in ((LATER, n - 1), (SCORED, n)) if m in slots]


def head_out(n):
    return ORDER[n // G], n % G


def raw_dmas(slot, s):
    return s + 1 + (slot == 1) * (s >= MIX0) + (s >= MIX0 + 1)


def build(nc, a, out):
    ctx = ExitStack()
    with ctx:
        def sb(name, shape, dt=F32):
            return ctx.enter_context(nc.sbuf_tensor(name, shape, dt))

        def sem(name):
            return ctx.enter_context(nc.semaphore(name))

        x = sb("x", [P, KD, T])
        xg_hi = sb("xg_hi", [P, KD, T], F32R)
        xg_lo = sb("xg_lo", [P, KD, T], F32R)
        raw = [sb(f"raw{r}", [P, KD * BLK]) for r in range(2)]
        hi = [sb(f"panel_hi{p}", [P, 8 * P], F32R) for p in range(4)]
        lo = [sb(f"panel_lo{p}", [P, 8 * P], F32R) for p in range(4)]
        rs = sb("rs", [P, T])
        tmp = [sb(f"tmp{j}", [P, T]) for j in range(2)]
        act = [sb(f"act{j}", [P, T]) for j in range(2)]
        sel = sb("sel", [P, G, P], F32R)
        dec = sb("dec", [P, T], F32R)
        tab = [sb(f"tab{j}", [P, T]) for j in range(2)]
        causal = sb("causal", [P, T])
        ident = sb("ident", [P, P])
        ones = sb("ones", [P, P])
        gain = sb("gain", [P, 62])
        neg_max = sb("neg_max", [P, 2, QT])
        row_sum = sb("row_sum", [P, 4, QT])
        inv_sum = sb("inv_sum", [P, 2, QT])
        fbias = sb("fbias", [P, DEPTH])
        gate = sb("gate", [P, T])
        sel_col = sb("sel_col", [P, G])

        start = -(-nc.sbuf_base // 32) * 32
        sb("region", [P, 2 * KF * T])

        def at(name, offset, shape, dt=F32):
            return nc.alloc_sbuf_tensor_at(name, shape, dt, offset=start + 4 * offset)

        x_rows = at("x_rows", 0, [P, QT, D])
        y_rows = at("y_rows", 0, [P, QT, D])
        gain_rows = at("gain_rows", QT * D, [P, P])
        a_hi = at("a_hi", 0, [P, KF, T], F32R)
        a_lo = at("a_lo", KF * T, [P, KF, T], F32R)
        mix_hi = at("mix_hi", 0, [P, KD, T], F32R)
        mix_lo = at("mix_lo", KD * T, [P, KD, T], F32R)
        lat = at("lat", 0, [P, 3, T])
        lat_hi = at("lat_hi", 3 * T, [P, 3, T], F32R)
        lat_lo = at("lat_lo", 6 * T, [P, 3, T], F32R)
        lat_sq = at("lat_sq", 9 * T, [P, 3, T])
        lat_rs = at("lat_rs", 12 * T, [P, 2, T])
        rot = at("rot", 14 * T, [P, 2, T])
        o1 = 2 * KD * T
        q1 = at("q1", o1, [P, G, T])
        k1 = at("k1", o1 + 4 * T, [P, G, T])
        v1 = at("v1", o1 + 8 * T, [P, QT, HW])
        q2 = at("q2", o1 + 10 * T, [P, 2, T])
        k2 = at("k2", o1 + 12 * T, [P, 2, T])
        v2 = at("v2", o1 + 14 * T, [P, QT, HW])
        o2 = o1 + 16 * T
        prob = [at(f"prob{j}", o2 + j * TRI[QT], [P, TRI[QT]]) for j in range(2)]
        probT = [at(f"probT{j}", o2 + (2 + j) * TRI[QT], [P, TRI[QT]]) for j in range(2)]
        o_rows = at("o_rows", o2 + 4 * TRI[QT], [P, QT, HW])
        QKV = {"C": (q1, k1, v1), "B": (q1, k1, v1), "A": (q2, k2, v2), "D": (q2, k2, v2)}
        k_misc = at("k_misc", o1 + 14 * T, [P, T])
        k_rot = at("k_rot", o1 + 15 * T, [P, T])

        bank = [ctx.enter_context(nc.psum_tensor(f"bank{b}", [P, T], F32)) for b in range(8)]
        S_BANK, PT_EVEN, PT_ODD, O_BANK, SMALL = (2, 3), bank[4], bank[5], bank[6], bank[7]
        WO_BANK = (0, 1, 3, 4)

        consts_in = sem("consts_in")
        x_in = sem("x_in")
        setup_done = sem("setup_done")
        gain_full = sem("gain_full")
        turned = sem("turned")
        raw_in = [sem(f"raw_in{r}") for r in range(2)]
        hi_ready = sem("hi_ready")
        lo_ready = sem("lo_ready")
        panel_used = sem("panel_used")
        out_free = sem("out_free")
        up_full = sem("up_full")
        x_ready = sem("x_ready")
        xg_hi_ready = sem("xg_hi_ready")
        xg_lo_ready = sem("xg_lo_ready")
        sq_ready = sem("sq_ready")
        sq_summed = sem("sq_summed")
        small_full = sem("small_full")
        small_free = sem("small_free")
        ln_done = sem("ln_done")
        guess = sem("guess")
        newton = sem("newton")
        rs_ready = sem("rs_ready")
        gated = sem("gated")
        silu_ready = sem("silu_ready")
        silu_scaled = sem("silu_scaled")
        a_ready = sem("a_ready")
        a_hi_ready = sem("a_hi_ready")
        a_lo_ready = sem("a_lo_ready")
        lat_sq_ready = sem("lat_sq_ready")
        lat_hi_ready = sem("lat_hi_ready")
        lat_lo_ready = sem("lat_lo_ready")
        lat_summed = sem("lat_summed")
        rope_in = sem("rope_in")
        rope_mul = sem("rope_mul")
        rope_done = sem("rope_done")
        tab_in = [sem(f"tab_in{j}") for j in range(2)]
        gate_step = sem("gate_step")
        gate_exp = sem("gate_exp")
        s_full = sem("s_full")
        logits_ready = sem("logits_ready")
        exp_ready = sem("exp_ready")
        pt_full = sem("pt_full")
        pt_even = sem("pt_even")
        pt_odd = sem("pt_odd")
        o_full = sem("o_full")
        inv_ready = sem("inv_ready")
        o_ready = sem("o_ready")
        mix_hi_ready = sem("mix_hi_ready")
        z_ready = sem("z_ready")
        z_turned = sem("z_turned")
        y_ready = sem("y_ready")
        y_out = sem("y_out")

        block = ctx.enter_context(nc.Block())

        def rawv(r, k, lo_col, n):
            return raw[r][:, 0:k * BLK].rearrange("p (k c) -> p k c", c=BLK)[:, :, lo_col:lo_col + n]

        def pan(buf, k, n=P):
            return buf[:, 0:k * n].rearrange("p (k c) -> p k c", c=n)

        def pieces(s, p):
            r, half = p // 2, P * (p % 2)
            if MIX0 <= s < FFN2:
                m = s - MIX0
                if (m, p) == (0, 3):
                    v, H = KV_RANK, ROPE // 2
                    return [((0, ROPE), rawv(r, KD, v, ROPE)), ((ROPE, ROPE + H), rawv(r, KD, v + H, H)),
                            ((ROPE + H, 2 * ROPE), rawv(r, KD, v, H)),
                            ((2 * ROPE, 2 * ROPE + G), rawv(r, KD, v + ROPE, G))]
                if m == 1 and p >= 2:
                    kq, nq, nk = Q_RANK // P, G * (HD + ROPE), G * 2 * HD
                    if p == 3:
                        w = raw[1][:, kq * nq:kq * nq + nk].rearrange("p (k h c) -> p k h c", k=1, h=G)
                        return [(("h", 1, 0, HD, 0, HD), w[:, :, :, 0:HD]),
                                (("h", 1, HW, HD, 0, HD), w[:, :, :, HD:2 * HD])]
                    w = raw[1][:, 0:kq * nq].rearrange("p (k h c) -> p k h c", k=kq, h=G)
                    H = ROPE // 2
                    return [(("h", kq, 0, HD, 0, HD), w[:, :, :, 0:HD]),
                            (("h", kq, HW, ROPE, 0, ROPE), w[:, :, :, HD:HD + ROPE]),
                            (("h", kq, HW + G * ROPE, ROPE, 0, H), w[:, :, :, HD + H:HD + ROPE]),
                            (("h", kq, HW + G * ROPE, ROPE, H, ROPE), w[:, :, :, HD:HD + H])]
                return [((0, P), rawv(r, KD, half, P))]
            d = s - GU_STEPS if s < MIX0 else s - FFN2 - GU_STEPS
            k = KD if d < 0 else DN_K[(2 * d + r) % 3]
            return [((0, P, k), rawv(r, k, half, P))]

        def place(buf, how, k=KD):
            if how[0] == "h":
                _, kq, c0, w, j0, j1 = how
                full = buf[:, 0:kq * 2 * HW].rearrange("p (k c) -> p k c", k=kq)[:, :, c0:c0 + G * w]
                return full.rearrange("p k (h c) -> p k h c", h=G)[:, :, :, j0:j1]
            k = how[2] if len(how) == 3 else k
            return pan(buf, k)[:, :, how[0]:how[1]]

        def each_piece(how, dst, src):
            if how[0] == "h":
                return [(dst(how)[:, k], src[:, k]) for k in range(how[1])]
            return [(dst(how), src)]

        @block.sync
        def _(sp):
            sp.dma_start(x_rows[:], a["x"].rearrange("o (q p) d -> p (o q) d", p=P)).then_inc(x_in, 16)
            n_rows = 0
            for l in range(DEPTH):
                for g in ("norm_ffn1", "norm_mix", "norm_ffn2"):
                    sp.dma_start(gain_rows[n_rows:n_rows + KD, :],
                                 a[g][l].rearrange("(k p) -> k p", p=P)).then_inc(consts_in, 16)
                    n_rows += KD
            sp.dma_start(gain_rows[n_rows:n_rows + KD, :],
                         a["norm_final"].rearrange("(k p) -> k p", p=P)).then_inc(consts_in, 16)
            sp.dma_start(gain_rows[56:60, :],
                         a["mla_q_norm"].rearrange("l (k p) -> (l k) p", p=P)).then_inc(consts_in, 16)
            sp.dma_start(gain_rows[60:62, :], a["mla_kv_norm"]).then_inc(consts_in, 16)
            sp.dma_start(ident[:], a["c_ident"]).then_inc(consts_in, 16)
            sp.dma_start(sel_col[:], a["c_sel"]).then_inc(consts_in, 16)
            sp.dma_start(causal[:], a["c_tables"][0]).then_inc(consts_in, 16)
            with nc.allow_non_contiguous_dma(reason="eight numbers"):
                sp.dma_start(fbias[2 * ROPE:2 * ROPE + G, :],
                             a["forget_bias"].rearrange("l g -> g l")).then_inc(consts_in, 16)

            def block_in(l, step, r, src, dst):
                sp.wait_ge(lo_ready, l * (4 * LAYER_STEPS) + step * 4 + 2 * r + 2)
                for d, s in zip(dst, src):
                    sp.dma_start(d, s).then_inc(raw_in[r], 16)

            def cols(w, l, c, n=BLK):
                tiles = w.shape[1] // P
                at_ = slice(c, c + n) if isinstance(c, int) else bass.ds(c, n)
                return w.rearrange("l (k p) n -> p (l k) n", p=P)[:, bass.ds(l * tiles, tiles), at_]

            def ffn_in(l, s0, name):
                with sp.Fori(0, GU_STEPS) as i:
                    for r, w in enumerate(("gate", "up")):
                        block_in(l, s0 + i, r, [cols(a[f"{name}_{w}"], l, i * BLK)], [rawv(r, KD, 0, BLK)])
                for b in range(3 * DN_PAIRS):
                    pair, third = b // 3, b % 3
                    src = cols(a[f"{name}_down"], l, pair * BLK)[:, 8 * third:8 * third + DN_K[third], :]
                    block_in(l, s0 + GU_STEPS + b // 2, b % 2, [src], [rawv(b % 2, DN_K[third], 0, BLK)])

            with sp.Fori(0, DEPTH) as l:
                ffn_in(l, 0, "ffn1")
                block_in(l, MIX0, 0, [cols(a["w_in"], l, CQ)], [rawv(0, KD, 0, BLK)])
                block_in(l, MIX0, 1, [cols(a["w_in"], l, CKV, KV_RANK + ROPE), cols(a["w_in"], l, BF, G)],
                         [rawv(1, KD, 0, KV_RANK + ROPE), rawv(1, KD, KV_RANK + ROPE, G)])
                block_in(l, MIX0 + 1, 0, [cols(a["w_in"], l, AQ)[:, 1:KD], cols(a["w_in"], l, AQ)[:, 0:1]],
                         [rawv(0, KD, 0, BLK)[:, 1:KD], rawv(0, KD, 0, BLK)[:, 0:1]])
                nq, nk = G * (HD + ROPE), G * 2 * HD
                block_in(l, MIX0 + 1, 1,
                         [a["w_uq"][bass.ds(l, 1)].rearrange("o (k p) n -> p (o k) n", p=P),
                          a["w_ukv"][bass.ds(l, 1)].rearrange("o p n -> p (o n)")],
                         [raw[1][:, 0:2 * nq].rearrange("p (k n) -> p k n", k=2),
                          raw[1][:, 2 * nq:2 * nq + nk]])
                for m in range(2, 6):
                    for r in range(2):
                        block_in(l, MIX0 + m, r, [cols(a["w_in"], l, MIX_COLS[m, r])], [rawv(r, KD, 0, BLK)])
                for m in range(6, 8):
                    for r in range(2):
                        block_in(l, MIX0 + m, r, [cols(a["w_out"], l, (2 * (m - 6) + r) * BLK)],
                                 [rawv(r, KD, 0, BLK)])
                ffn_in(l, FFN2, "ffn2")
            for d in range(KD):
                sp.wait_ge(y_ready, d + 1)
                sp.dma_start(out.rearrange("o (q p) d -> p (o q) d", p=P)[:, :, P * d:P * (d + 1)],
                             y_rows[:, :, P * d:P * (d + 1)]).then_inc(y_out, 16)
            sp.wait_ge(y_out, 16 * KD)

        @block.tensor
        def _(pe):
            pe.wait_ge(consts_in, 16 * 13)
            pe.transpose(SMALL[:, 0:62], gain_rows[0:62, :], ident[0:62, 0:62]).then_inc(gain_full, 1)
            pe.wait_ge(x_in, 16)
            for d in range(KD):
                if d >= 2:
                    pe.wait_ge(x_ready, d - 1)
                for q in range(QT):
                    last = pe.transpose(bank[d % 2][:, P * q:P * (q + 1)],
                                        x_rows[:, q, P * d:P * (d + 1)], ident[:])
                last.then_inc(turned, 1)
            pe.wait_ge(setup_done, 9)

            def panel_ready(l, step, p):
                pe.wait_ge(lo_ready, l * (4 * LAYER_STEPS) + step * 4 + p + 5)

            def products(dst, p, k, rhs_hi, rhs_lo, first, last, col=0, n=P, width=P, k0=0, kp=0):
                w_hi, w_lo = pan(hi[p], kp + k, width), pan(lo[p], kp + k, width)
                for j in range(k):
                    for t, (w, v) in enumerate(((w_hi, rhs_hi), (w_hi, rhs_lo), (w_lo, rhs_hi))):
                        mm = pe.matmul(dst, w[:, kp + j, col:col + n], v[:, k0 + j, :],
                                       start=first and j == 0 and t == 0, stop=last and j == k - 1 and t == 2)
                return mm

            def small_use(l, u):
                if u:
                    pe.wait_ge(small_free, l * LAYER_USES + u)

            def sum_squares(l, u, src):
                small_use(l, u)
                pe.matmul(SMALL[:], ones[:], src, start=True, stop=True).then_inc(small_full, 1)

            def first_products(l, nth, dst, p):
                pe.wait_ge(x_ready, l * LAYER_X + KD * nth + KD - 1)
                for j in range(KD):
                    pe.wait_ge(xg_lo_ready, l * LAYER_X + KD * nth + j + 1)
                    mm = products(dst, p, 1, xg_hi, xg_lo, j == 0, j == KD - 1, k0=j, kp=j)
                return mm

            def ffn(l, s0, nth, use):
                def gate_up(i, first=False):
                    for p in range(4):
                        panel_ready(l, s0 + i, p)
                        if not first:
                            pe.wait_ge(gated if p < 2 else a_ready,
                                       l * (2 * KF) + (KF if s0 else 0) + i * 2 + p % 2 - 1)
                        if first and p == 0:
                            mm = first_products(l, nth, bank[p][:], p)
                        else:
                            mm = products(bank[p][:], p, KD, xg_hi, xg_lo, True, True)
                        mm.then_inc(panel_used, 1)
                        if first and p == 0:
                            pe.wait_ge(sq_summed, (l * 3 + nth + 1) * (KD - 1))
                            sum_squares(l, use, act[0][:])

                gate_up(0, first=True)
                with pe.Fori(1, GU_STEPS) as i:
                    gate_up(i)
                for b in range(3 * DN_PAIRS):
                    pair, third = b // 3, b % 3
                    if pair == 0:
                        pe.wait_ge(a_lo_ready, l * (2 * KF) + (KF if s0 else 0) + 8 * third + DN_K[third])
                    for h in range(2):
                        p = 2 * (b % 2) + h
                        panel_ready(l, s0 + GU_STEPS + b // 2, p)
                        if third == 0 and pair:
                            pe.wait_ge(x_ready, l * LAYER_X + KD * (nth + 1) + 2 * pair + h - 1)
                        products(bank[4 + h][:], p, DN_K[third], a_hi, a_lo, third == 0, third == 2,
                                 k0=8 * third).then_inc(panel_used, 1)

            def project(l, m, p, ks=range(KD)):
                j = mix_out(m, p)
                b, former = out_bank(j)
                n = 2 * ROPE + G if (m, p) == (0, 3) else P
                if ks[0] == 0:
                    panel_ready(l, MIX0 + m, p)
                    if former >= 0:
                        pe.wait_ge(out_free, l * MIX_OUTS + former + 1)
                mm = products(bank[b][0:n, :], p, len(ks), xg_hi, xg_lo, ks[0] == 0, ks[-1] == KD - 1, n=n,
                              k0=ks[0], kp=ks[0])
                if ks[-1] == KD - 1:
                    mm.then_inc(panel_used, 1)

            def project_out(l, d, ks):
                p = d % 4
                if ks[0] == 0:
                    panel_ready(l, MIX0 + 6 + d // 4, p)
                    if d >= 4:
                        pe.wait_ge(x_ready, l * LAYER_X + 2 * KD + d - 3)
                mm = products(bank[WO_BANK[p]][:], p, len(ks), mix_hi, mix_lo, ks[0] == 0, ks[-1] == KD - 1,
                              k0=ks[0], kp=ks[0])
                if ks[-1] == KD - 1:
                    mm.then_inc(panel_used, 1)

            def up_project(l, p):
                panel_ready(l, MIX0 + 1, p)
                k0, k = (0, Q_RANK // P) if p == 2 else (Q_RANK // P, 1)
                pe.wait_ge(lat_lo_ready, l * 3 + k0 + k)
                for o in range(4):
                    b, former = out_bank(mix_out(1, p, o))
                    pe.wait_ge(out_free, l * MIX_OUTS + former + 1)
                    mm = products(bank[b][:], p, k, lat_hi, lat_lo, True, True, col=P * o, width=2 * HW, k0=k0)
                    mm.then_inc(panel_used if o == 3 else up_full, 1)

            def queries_ready(l, n):
                mixer, h = head_out(n)
                if mixer == "C":
                    pe.wait_ge(rope_done, l * 8 + 8)
                    pe.wait_ge(out_free, l * MIX_OUTS + mix_out(1, 3, 1) + 1)
                else:
                    keys = next(sp_ for sp_, d in DEST.items() if d == f"k{mixer}{h // 2}")
                    pe.wait_ge(out_free, l * MIX_OUTS + mix_out(*keys) + 1)
                if n == 2 * G:
                    pe.wait_ge(gate_step, l * 9 + 9)

            def scores(l, n, i):
                mixer, h = head_out(n)
                q, k, _ = QKV[mixer]
                r0, rows, tile = (0, HD + ROPE, h) if mixer == "C" else (HD * (h % 2), HD, h // 2)
                e = 4 * n + i
                if i == 0:
                    queries_ready(l, n)
                if e >= 2:
                    pe.wait_ge(logits_ready, l * (4 * HEADS) + e - 1)
                w = P * (i + 1)
                dst = bank[S_BANK[i % 2]][:, 0:w]
                if mixer == "B":
                    pe.matmul(dst, sel[r0:r0 + 36, h, :], dec[r0:r0 + 36, 0:w], start=True, stop=False)
                pe.matmul(dst, q[r0:r0 + rows, tile, P * i:P * (i + 1)], k[r0:r0 + rows, tile, 0:w],
                          start=mixer != "B", stop=True).then_inc(s_full, 1)

            def turn_probs(l, n, kts):
                for kt in kts:
                    for i in range(kt, QT):
                        dst, c = (PT_ODD, TRT[kt] - TRT[1] - P * kt) if kt % 2 else (PT_EVEN, 0)
                        last = pe.transpose(dst[:, c + P * i:c + P * (i + 1)],
                                            prob[n % 2][:, TRI[i] + P * kt:TRI[i] + P * (kt + 1)], ident[:])
                last.then_inc(pt_full, 1)

            def weigh_values(l, n):
                mixer, h = head_out(n)
                v = QKV[mixer][2]
                pe.wait_ge(pt_even, l * (2 * HEADS) + 2 * n + 2)
                pe.wait_ge(pt_odd, l * HEADS + n + 1)
                if h == 0:
                    pe.wait_ge(small_free, l * LAYER_USES + U_VT[mixer] + 2)
                if n:
                    pe.wait_ge(o_ready, l * HEADS + n)
                for i in range(QT):
                    for kt in range(i + 1):
                        c = TRT[kt] + P * (i - kt)
                        last = pe.matmul(O_BANK[:, HD * i:HD * (i + 1)], probT[n % 2][:, c:c + P],
                                         v[:, kt, HD * h:HD * (h + 1)], start=kt == 0, stop=kt == i)
                last.then_inc(o_full, 1)

            def turn_values(l, mixer, pair):
                if mixer == "C":
                    done = mix_out(1, 3, 2 + pair)
                else:
                    done = mix_out(*next(k_ for k_, d in DEST.items() if d == f"v{mixer}{pair}"))
                pe.wait_ge(out_free, l * MIX_OUTS + done + 1)
                small_use(l, U_VT[mixer] + pair)
                for q in range(QT):
                    last = pe.transpose(SMALL[:, P * q:P * (q + 1)], tmp[pair][:, P * q:P * (q + 1)], ident[:])
                last.then_inc(small_full, 1)

            def turn_outputs(l, mixer, pair, dst=SMALL):
                pe.wait_ge(o_ready, l * HEADS + G * (ORDER.index(mixer) + 1))
                if dst is SMALL:
                    small_use(l, U_OT[mixer] + pair)
                for q in range(QT):
                    last = pe.transpose(dst[:, P * q:P * (q + 1)],
                                        o_rows[:, q, P * pair:P * (pair + 1)], ident[:])
                last.then_inc(small_full, 1)

            def turn(l, n, pair):
                if n in SLOT_VT:
                    turn_values(l, SLOT_VT[n], pair)
                if n in SLOT_OT:
                    turn_outputs(l, SLOT_OT[n], pair)

            def attend(l, n):
                if 1 <= n <= HEADS:
                    pe.wait_ge(exp_ready, l * (4 * HEADS) + 4 * n)
                    if n >= 2:
                        pe.wait_ge(pt_even, l * (2 * HEADS) + 2 * (n - 1))
                    turn_probs(l, n - 1, [0])
                    if n >= 2:
                        pe.wait_ge(pt_odd, l * HEADS + n - 1)
                    turn_probs(l, n - 1, [1, 3])
                if n >= 2:
                    weigh_values(l, n - 2)
                if 1 <= n <= HEADS:
                    pe.wait_ge(pt_even, l * (2 * HEADS) + 2 * (n - 1) + 1)
                    turn_probs(l, n - 1, [2])

            with pe.Fori(0, DEPTH) as l:
                ffn(l, 0, 0, U_FFN1)
                panel_ready(l, MIX0, 0)
                first_products(l, 1, bank[0][:], 0).then_inc(panel_used, 1)
                pe.wait_ge(sq_summed, (l * 3 + 2) * (KD - 1))
                sum_squares(l, U_MIX, act[0][:])
                for p in (1, 2, 3):
                    project(l, 0, p)
                pe.wait_ge(lat_summed, l + 1)
                sum_squares(l, U_LQ, lat_sq[:, 0, :])
                project(l, 1, 0)
                pe.wait_ge(lat_sq_ready, l * 3 + 3)
                sum_squares(l, U_LKV, lat_sq[:, 2, :])
                project(l, 1, 1)
                up_project(l, 2)
                up_project(l, 3)
                project(l, 2, 0)
                for n in range(HEADS):
                    for i in range(QT):
                        if n in SCORED:
                            project(l, *SCORED[n], ks=range(2 * i, 2 * i + 2))
                        scores(l, n, i)
                    turn(l, n, 0)
                    attend(l, n)
                    turn(l, n, 1)
                    if n in LATER:
                        project(l, *LATER[n])
                early, late = range(0, ROWS["D"]), range(ROWS["D"], KD)
                project_out(l, 0, early)
                attend(l, HEADS)
                project_out(l, 1, early)
                attend(l, HEADS + 1)
                project_out(l, 2, early)
                turn_outputs(l, "D", 0)
                turn_outputs(l, "D", 1, bank[2])
                project_out(l, 3, early)
                pe.wait_ge(small_free, l * LAYER_USES + U_OT["D"] + 2)
                for d in range(4):
                    project_out(l, d, late)
                for d in range(4, KD):
                    project_out(l, d, range(KD))
                ffn(l, FFN2, 2, U_FFN2)
            pe.wait_ge(sq_summed, (3 * DEPTH + 1) * (KD - 1))
            pe.wait_ge(small_free, DEPTH * LAYER_USES)
            pe.matmul(SMALL[:], ones[:], act[0][:], start=True, stop=True).then_inc(small_full, 1)
            for d in range(KD):
                pe.wait_ge(z_ready, d + 1)
                if d >= 2:
                    pe.wait_ge(y_ready, d - 1)
                for q in range(QT):
                    last = pe.transpose(bank[d % 2][:, P * q:P * (q + 1)], tmp[d % 2][:, P * q:P * (q + 1)], ident[:])
                last.then_inc(z_turned, 1)

        @block.scalar
        def _(sc):
            def split_hi(l, s, p, step=None):
                step = s if step is None else step
                sc.wait_ge(panel_used, l * (4 * LAYER_STEPS) + step * 4 + p + 1)
                r = p // 2
                sc.wait_ge(raw_in[r], l * (16 * raw_dmas(r, LAYER_STEPS - 1)) + step * 16
                           + 16 * (raw_dmas(r, s) - s))
                for how, src in pieces(s, p):
                    for d, v in each_piece(how, lambda h_: place(hi[p], h_), src):
                        last = sc.activation(d, v, ACT.Copy)
                last.then_inc(hi_ready, 1)

            def x_tile(m, d, g):
                sc.wait_ge(x_ready, m * KD + d + 1)
                sc.activation(xg_hi[:, d, :], x[:, d, :], ACT.Copy, scale=gain[:, g]).then_inc(xg_hi_ready, 1)
                if d >= 3:
                    sc.wait_ge(sq_summed, m * (KD - 1) + d - 2)
                sc.activation((tmp[d % 2] if d else act[0])[:], x[:, d, :], ACT.Square).then_inc(sq_ready, 1)

            def norm_guess(l, n):
                c = l * NORMS + n
                use = (U_FFN1, U_MIX, U_LQ, U_LKV, U_FFN2)[n]
                sc.wait_ge(small_free, l * LAYER_USES + use + 1)
                sc.activation(tmp[1][:], tmp[0][:], ACT.Ln).then_inc(ln_done, 1)
                sc.wait_ge(ln_done, c + 1)
                sc.activation(tmp[1][:], tmp[1][:], ACT.Exp, scale=-0.5).then_inc(guess, 1)

            def ffn(l, s0, nth, nrm, after):
                def gate_up(i, following, step, first=False):
                    for p in range(4):
                        split_hi(l, following, p, step)
                        f = l * (2 * KF) + (KF if s0 else 0) + i * 2 + p % 2 + 1
                        if first and p == 0:
                            norm_guess(l, nrm)
                        if p < 2:
                            sc.wait_ge(gated, f)
                            sc.activation(tmp[p][:], tmp[p][:], ACT.Silu).then_inc(silu_ready, 1)
                        else:
                            sc.wait_ge(a_ready, f)
                            sc.activation(a_hi[:, bass.ds(i * 2 + p - 2, 1), :],
                                          act[p - 2][:].unsqueeze(1), ACT.Copy).then_inc(a_hi_ready, 1)

                gate_up(0, s0, s0 + 1, first=True)
                with sc.Fori(1, GU_STEPS - 1) as i:
                    gate_up(i, s0, s0 + i + 1)
                gate_up(GU_STEPS - 1, s0 + GU_STEPS, s0 + GU_STEPS)
                for b in range(3 * DN_PAIRS):
                    s = s0 + GU_STEPS + b // 2
                    for h in range(2):
                        if s + 1 < s0 + FFN_STEPS or after:
                            split_hi(l, s + 1, 2 * (b % 2) + h)
                        if b % 3 == 2:
                            d = 2 * (b // 3) + h
                            x_tile(l * 3 + nth + 1, d, gain_at(l, nth + 1, d))

            def gain_at(l, g, d):
                return bass.ds(l * (3 * KD) + g * KD + d, 1)

            def copy_pt(l, n):
                sc.wait_ge(pt_full, l * (3 * HEADS) + 3 * n + 2)
                if n >= 2:
                    sc.wait_ge(o_full, l * HEADS + n - 1)
                sc.activation(probT[n % 2][:, TRT[1]:TRT[1] + T], PT_ODD[:], ACT.Copy).then_inc(pt_odd, 1)

            def outputs_hi(l, mixer, pair, src=SMALL):
                sc.wait_ge(small_full, l * LAYER_USES + U_OT[mixer] + pair + 1)
                sc.activation(mix_hi[:, ROWS[mixer] + pair, :], src[:], ACT.Copy).then_inc(mix_hi_ready, 1)

            def table_in(which, j):
                sc.dma_start(tab[j][:], a["c_tables"][which]).then_inc(tab_in[j], 16)

            def latent(l, j):
                sc.wait_ge(out_free, l * MIX_OUTS + j + 1)
                sc.activation(lat_sq[:, j, :], lat[:, j, :], ACT.Square).then_inc(lat_sq_ready, 1)
                g = l * 2 + 56 + j if j < 2 else l + 60
                sc.activation(lat_hi[:, j, :], lat[:, j, :], ACT.Copy,
                              scale=gain[:, bass.ds(g, 1)]).then_inc(lat_hi_ready, 1)

            sc.wait_ge(setup_done, 9)
            for d in range(KD):
                x_tile(0, d, slice(d, d + 1))
            with sc.Fori(0, DEPTH) as l:
                for p in range(4):
                    split_hi(l, 0, p)
                ffn(l, 0, 0, N_FFN1, True)
                table_in(1, 0)
                table_in(2, 1)
                for p in range(4):
                    split_hi(l, MIX0 + 1, p)
                    if p == 0:
                        norm_guess(l, N_MIX)
                    if p < 3:
                        latent(l, p)
                split_hi(l, MIX0 + 2, 0)
                norm_guess(l, N_LQ)
                split_hi(l, MIX0 + 2, 1)
                norm_guess(l, N_LKV)
                split_hi(l, MIX0 + 2, 2)
                split_hi(l, MIX0 + 2, 3)
                split_hi(l, MIX0 + 3, 0)
                for n in range(HEADS + 1):
                    if n < HEADS:
                        for i in range(QT):
                            sc.wait_ge(logits_ready, l * (4 * HEADS) + 4 * n + i + 1)
                            pr = prob[n % 2][:, TRI[i]:TRI[i + 1]]
                            sc.activation(pr, pr, ACT.Exp, scale=-1.0, bias=neg_max[:, n % 2, i:i + 1],
                                          accum_out=row_sum[:, n % 4, i:i + 1]).then_inc(exp_ready, 1)
                        if ORDER[min(n + 2, HEADS - 1) // G] in "AD" and n + 2 < HEADS:
                            mixer, h = head_out(n + 2)
                            table_in((3 if mixer == "A" else 7) + h, n % 2)
                    if n in SLOT_OT:
                        outputs_hi(l, SLOT_OT[n], 0)
                    if n:
                        copy_pt(l, n - 1)
                    for m, p in freed_panels(n):
                        split_hi(l, MIX0 + m + 1, p)
                    if n == 1:
                        sc.wait_ge(gate_step, l * 9 + 2)
                        g_ = gate[0:G, :]
                        sc.activation(g_, g_, ACT.Exp).then_inc(gate_exp, 1)
                        sc.wait_ge(gate_exp, l * 2 + 1)
                        sc.activation(g_, g_, ACT.Ln, bias=ones[0:G, 0:1]).then_inc(gate_exp, 1)
                    if n in SLOT_OT:
                        outputs_hi(l, SLOT_OT[n], 1)
                outputs_hi(l, "D", 0)
                outputs_hi(l, "D", 1, bank[2])
                for m in (6, 7):
                    for p in range(4):
                        split_hi(l, MIX0 + m + 1, p)
                        d = 4 * (m - 6) + p
                        x_tile(l * 3 + 2, d, gain_at(l, 2, d))
                ffn(l, FFN2, 2, N_FFN2, False)
            norm_guess(DEPTH, N_FFN1)
            for d in range(KD):
                sc.wait_ge(z_turned, d + 1)
                sc.activation(y_rows[:, :, P * d:P * (d + 1)],
                              bank[d % 2][:].rearrange("p (q c) -> p q c", q=QT), ACT.Copy).then_inc(y_ready, 1)

        @block.gpsimd
        def _(po):
            def add_squares(m):
                for d in range(1, KD):
                    po.wait_ge(sq_ready, m * KD + d + 1)
                    if d > 1:
                        po.wait_ge(sq_summed, m * (KD - 1) + d - 1)
                    po.tensor_tensor(act[0][:], act[0][:], tmp[d % 2][:], ALU.add).then_inc(sq_summed, 1)

            def ffn(l, second, nth, nrm):
                with po.Fori(0, GU_STEPS) as i:
                    for j in range(2):
                        po.wait_ge(rs_ready, l * NORMS + nrm + 1)
                        po.wait_ge(silu_ready, l * (2 * KF) + (KF if second else 0) + i * 2 + j + 1)
                        po.tensor_tensor(tmp[j][:], tmp[j][:], rs[:], ALU.mult).then_inc(silu_scaled, 1)
                add_squares(l * 3 + nth + 1)

            add_squares(0)
            with po.Fori(0, DEPTH) as l:
                ffn(l, False, 0, N_FFN1)
                po.wait_ge(lat_sq_ready, l * 3 + 2)
                po.tensor_tensor(lat_sq[:, 0, :], lat_sq[:, 0, :], lat_sq[:, 1, :], ALU.add).then_inc(lat_summed, 1)
                for j in range(2):
                    po.wait_ge(out_free, l * MIX_OUTS + mix_out(1, 2, 2 + j) + 1)
                    po.wait_ge(tab_in[j], l * 80 + 16)
                    po.tensor_tensor(rot[:, j, :], rot[:, j, :], tab[j][:], ALU.mult).then_inc(rope_mul, 1)
                add_squares(l * 3 + 2)
                ffn(l, True, 2, N_FFN2)

        @block.vector
        def _(dv):
            def split_lo(l, s, p, step=None):
                step = s if step is None else step
                dv.wait_ge(hi_ready, l * (4 * LAYER_STEPS) + step * 4 + p + 1)
                for how, src in pieces(s, p):
                    for (d, v), (h_, _) in zip(each_piece(how, lambda q: place(lo[p], q), src),
                                               each_piece(how, lambda q: place(hi[p], q), src)):
                        last = dv.tensor_tensor(d, v, h_.bitcast(F32), ALU.subtract)
                last.then_inc(lo_ready, 1)

            def x_lo(nth, d, g):
                dv.wait_ge(xg_hi_ready, nth + 1)
                dv.scalar_tensor_tensor(xg_lo[:, d, :], x[:, d, :], gain[:, g], xg_hi[:, d, :].bitcast(F32),
                                        ALU.mult, ALU.subtract).then_inc(xg_lo_ready, 1)

            def x_tile(l, src, nth, d, g, half):
                dv.scalar_tensor_tensor(x[:, d, :], src[:], half, x[:, d, :], ALU.mult, ALU.add
                                        ).then_inc(x_ready, 1)
                x_lo(nth, d, g)

            def gain_at(l, g, d):
                return bass.ds(l * (3 * KD) + g * KD + d, 1)

            def norm(l, n, width, dst):
                c = l * NORMS + n
                use = (U_FFN1, U_MIX, U_LQ, U_LKV, U_FFN2)[n]
                dv.wait_ge(small_full, l * LAYER_USES + use + 1)
                dv.tensor_scalar(tmp[0][:], SMALL[:], 1.0 / width, EPS, ALU.mult, ALU.add).then_inc(small_free, 1)
                dv.wait_ge(guess, c + 1)
                dv.tensor_tensor(act[1][:], tmp[1][:], tmp[1][:], ALU.mult).then_inc(newton, 1)
                dv.wait_ge(newton, c * 2 + 1)
                dv.scalar_tensor_tensor(act[1][:], act[1][:], -0.5, tmp[0][:], ALU.mult, ALU.mult).then_inc(newton, 1)
                dv.wait_ge(newton, c * 2 + 2)
                dv.scalar_tensor_tensor(dst, act[1][:], 1.5, tmp[1][:], ALU.add, ALU.mult).then_inc(rs_ready, 1)
                dv.wait_ge(rs_ready, c + 1)

            def panel_done(l, step, p):
                dv.wait_ge(panel_used, l * (4 * LAYER_STEPS) + step * 4 + p + 5)

            def ffn(l, s0, nth, nrm, after):
                def gate_up(i, following, step, first=False):
                    for p in range(4):
                        if first and p == 0:
                            norm(l, nrm, D, rs[:])
                        j, f = p % 2, l * (2 * KF) + (KF if s0 else 0) + i * 2 + p % 2 + 1
                        panel_done(l, s0 + i, p)
                        if p < 2:
                            dv.tensor_tensor(tmp[j][:], bank[p][:], rs[:], ALU.mult).then_inc(gated, 1)
                        else:
                            dv.wait_ge(silu_scaled, f)
                            dv.tensor_tensor(act[j][:], bank[p][:], tmp[j][:], ALU.mult).then_inc(a_ready, 1)
                        split_lo(l, following, p, step)
                        if p >= 2:
                            dv.wait_ge(a_hi_ready, f)
                            dv.tensor_tensor(a_lo[:, bass.ds(i * 2 + j, 1), :], act[j][:].unsqueeze(1),
                                             a_hi[:, bass.ds(i * 2 + j, 1), :].bitcast(F32),
                                             ALU.subtract).then_inc(a_lo_ready, 1)

                gate_up(0, s0, s0 + 1, first=True)
                with dv.Fori(1, GU_STEPS - 1) as i:
                    gate_up(i, s0, s0 + i + 1)
                gate_up(GU_STEPS - 1, s0 + GU_STEPS, s0 + GU_STEPS)
                for b in range(3 * DN_PAIRS):
                    s = s0 + GU_STEPS + b // 2
                    for h in range(2):
                        p = 2 * (b % 2) + h
                        if b % 3 == 2:
                            panel_done(l, s, p)
                            d = 2 * (b // 3) + h
                            x_tile(l, bank[4 + h], l * LAYER_X + KD * (nth + 1) + d, d, gain_at(l, nth + 1, d), 0.5)
                        if s + 1 < s0 + FFN_STEPS or after:
                            split_lo(l, s + 1, p)

            def emptied(l, o, dst, src, by):
                dv.tensor_tensor(dst, src, by, ALU.mult).then_inc(out_free, 1)

            def values_turned(l, mixer, pair):
                dv.wait_ge(small_full, l * LAYER_USES + U_VT[mixer] + pair + 1)
                dv.tensor_copy(QKV[mixer][2][:, :, P * pair:P * (pair + 1)],
                               SMALL[:].rearrange("p (q c) -> p q c", q=QT)).then_inc(small_free, 1)

            def outputs_lo(l, mixer, pair, src=SMALL):
                dv.wait_ge(mix_hi_ready, l * KD + 2 * ORDER.index(mixer) + pair + 1)
                row = ROWS[mixer] + pair
                dv.tensor_tensor(mix_lo[:, row, :], src[:], mix_hi[:, row, :].bitcast(F32), ALU.subtract
                                 ).then_inc(small_free, 1)

            def turned_in_slot(l, n, pair):
                if n in SLOT_VT:
                    values_turned(l, SLOT_VT[n], pair)
                if n in SLOT_OT:
                    outputs_lo(l, SLOT_OT[n], pair)

            def latents_and_rotary_key(l):
                for p in range(4):
                    if p == 0:
                        norm(l, N_MIX, D, rs[:])
                    panel_done(l, MIX0, p)
                    if p < 3:
                        emptied(l, p, lat[:, p, :], bank[p][:], rs[:])
                        split_lo(l, MIX0 + 1, p)
                        dv.wait_ge(lat_hi_ready, l * 3 + p + 1)
                        g = l * 2 + 56 + p if p < 2 else l + 60
                        dv.scalar_tensor_tensor(lat_lo[:, p, :], lat[:, p, :], gain[:, bass.ds(g, 1)],
                                                lat_hi[:, p, :].bitcast(F32), ALU.mult, ALU.subtract
                                                ).then_inc(lat_lo_ready, 1)
                    else:
                        n = 2 * ROPE + G
                        emptied(l, p, k_misc[0:n, :], bank[p][0:n, :], rs[0:n, :])
                        split_lo(l, MIX0 + 1, p)
                        dv.wait_ge(out_free, l * MIX_OUTS + p + 1)
                        for j in range(2):
                            dv.wait_ge(tab_in[j], l * 80 + 16)
                        dv.tensor_tensor(k_rot[0:ROPE, :], k_misc[0:ROPE, :], tab[0][0:ROPE, :], ALU.mult
                                         ).then_inc(rope_in, 1)
                        dv.tensor_tensor(gate[0:ROPE, :], k_misc[ROPE:2 * ROPE, :], tab[1][ROPE:2 * ROPE, :], ALU.mult
                                         ).then_inc(rope_in, 1)
                        dv.wait_ge(rope_in, l * 2 + 2)
                        for h in range(G):
                            dv.tensor_tensor(k1[HD:HD + ROPE, h, :], k_rot[0:ROPE, :], gate[0:ROPE, :], ALU.add
                                             ).then_inc(rope_done, 1)

            def up_projections(l):
                for p in (2, 3):
                    by, dst = lat_rs[:, p - 2, :], (q1, k1)[p - 2]
                    for o in range(4):
                        j = mix_out(1, p, o)
                        src = bank[out_bank(j)[0]]
                        if o < 3:
                            dv.wait_ge(up_full, l * 6 + 3 * (p - 2) + o + 1)
                        else:
                            panel_done(l, MIX0 + 1, p)
                        if o < 2:
                            dv.tensor_tensor(dst[0:HD, 2 * o, :], src[0:HD, :], by[0:HD, :], ALU.mult)
                            emptied(l, j, dst[0:HD, 2 * o + 1, :], src[HD:P, :], by[HD:P, :])
                        elif p == 2:
                            emptied(l, j, rot[:, o - 2, :], src[:], by)
                        else:
                            emptied(l, j, tmp[o - 2][:], src[:], by)
                    split_lo(l, MIX0 + 2, p)
                dv.wait_ge(rope_mul, l * 2 + 2)
                for h in range(G):
                    r = slice(ROPE * h, ROPE * (h + 1))
                    dv.tensor_tensor(q1[HD:HD + ROPE, h, :], rot[r, 0, :], rot[r, 1, :], ALU.add).then_inc(rope_done, 1)

            def project(l, m, p):
                panel_done(l, MIX0 + m, p)
                name = DEST[m, p]
                pair, (q, k, _) = int(name[2]), QKV[name[1]]
                dst = {"q": q, "k": k}[name[0]][:, pair, :] if name[0] != "v" else tmp[pair][:]
                emptied(l, mix_out(m, p), dst, bank[out_bank(mix_out(m, p))[0]][:], rs[:])

            def gates_in(l):
                dv.tensor_scalar(k_rot[0:G, :], k_misc[2 * ROPE:2 * ROPE + G, :],
                                 fbias[2 * ROPE:2 * ROPE + G, bass.ds(l, 1)], None, ALU.add).then_inc(gate_step, 1)
                dv.wait_ge(gate_step, l * 9 + 1)
                dv.scalar_tensor_tensor(gate[0:G, :], k_rot[0:G, :], -1.0, k_rot[0:G, :], ALU.mult, ALU.min
                                        ).then_inc(gate_step, 1)

            def gates_out(l):
                dv.wait_ge(gate_exp, l * 2 + 2)
                dv.scalar_tensor_tensor(k_rot[0:G, :], k_rot[0:G, :], 0.0, gate[0:G, :], ALU.min, ALU.subtract
                                        ).then_inc(gate_step, 1)
                dv.wait_ge(gate_step, l * 9 + 3)
                dv.tensor_tensor_scan(gate[0:G, :], ones[0:G, 0:1].to_broadcast([G, T]), k_rot[0:G, :], 0.0,
                                      ALU.mult, ALU.add).then_inc(gate_step, 1)
                dv.wait_ge(gate_step, l * 9 + 4)
                dv.tensor_scalar(k_rot[0:G, :], gate[0:G, :], -1.0 / SCALE, None, ALU.mult).then_inc(gate_step, 1)
                dv.wait_ge(gate_step, l * 9 + 5)
                dv.tensor_copy(dec[0:G, :], k_rot[0:G, :]).then_inc(gate_step, 1)
                dv.tensor_copy(dec[64:64 + G, :], k_rot[0:G, :]).then_inc(gate_step, 1)
                dv.wait_ge(gate_step, l * 9 + 6)
                for r in (32, 96):
                    dv.tensor_tensor(dec[r:r + G, :], k_rot[0:G, :], dec[0:G, :].bitcast(F32), ALU.subtract
                                     ).then_inc(gate_step, 1)

            def logits(l, n, i):
                mixer, h = head_out(n)
                table, scale = causal, SCALE_MLA if mixer == "C" else SCALE
                if mixer in "AD":
                    table = tab[n % 2]
                dv.wait_ge(s_full, 4 * n + i + 1)
                w = P * (i + 1)
                dv.tensor_tensor_reduce(prob[n % 2][:, TRI[i]:TRI[i + 1]], bank[S_BANK[i % 2]][:, 0:w],
                                        table[:, T - w:T], -scale, BIG, ALU.add, ALU.min,
                                        neg_max[:, n % 2, i:i + 1]).then_inc(logits_ready, 1)

            def copy_pt(l, n, kt):
                dv.wait_ge(pt_full, l * (3 * HEADS) + 3 * n + (3 if kt else 1))
                if n >= 2:
                    dv.wait_ge(o_full, l * HEADS + n - 1)
                w = T - P * kt
                dv.tensor_copy(probT[n % 2][:, TRT[kt]:TRT[kt] + w], PT_EVEN[:, P * kt:T]).then_inc(pt_even, 1)

            def outputs(l, n):
                _, h = head_out(n)
                dv.wait_ge(o_full, l * HEADS + n + 1)
                dv.reciprocal(inv_sum[:, n % 2, :], row_sum[:, n % 4, :]).then_inc(inv_ready, 1)
                dv.wait_ge(inv_ready, l * HEADS + n + 1)
                dv.tensor_tensor(o_rows[:, :, HD * h:HD * (h + 1)],
                                 O_BANK[:, 0:QT * HD].rearrange("p (q c) -> p q c", q=QT),
                                 inv_sum[:, n % 2, :].unsqueeze(2).to_broadcast([P, QT, HD]),
                                 ALU.mult).then_inc(o_ready, 1)

            dv.memset(ones[:], 1.0).then_inc(setup_done, 1)
            dv.memset(dec[:].bitcast(F32), 0.0).then_inc(setup_done, 1)
            dv.memset(sel[:].bitcast(F32), 0.0).then_inc(setup_done, 1)
            dv.memset(inv_sum[:], 0.0).then_inc(panel_used, 4)
            dv.memset(neg_max[:], 0.0).then_inc(lo_ready, 4)
            dv.wait_ge(consts_in, 16 * 13)
            dv.wait_ge(setup_done, 3)
            for r in range(0, P, 32):
                dv.tensor_copy(sel[r:r + G, :, :], sel_col[r:r + G, :].unsqueeze(2).to_broadcast([G, G, P])
                               ).then_inc(setup_done, 1)
            dv.memset(row_sum[:], 0.0).then_inc(setup_done, 1)
            dv.wait_ge(gain_full, 1)
            dv.tensor_copy(gain[:], SMALL[:, 0:62]).then_inc(setup_done, 1)
            dv.wait_ge(setup_done, 9)
            for d in range(KD):
                dv.wait_ge(turned, d + 1)
                dv.tensor_copy(x[:, d, :], bank[d % 2][:]).then_inc(x_ready, 1)
                x_lo(d, d, slice(d, d + 1))
            with dv.Fori(0, DEPTH) as l:
                for p in range(4):
                    split_lo(l, 0, p)
                ffn(l, 0, 0, N_FFN1, True)
                latents_and_rotary_key(l)
                for p, (n, rank) in enumerate(((N_LQ, Q_RANK), (N_LKV, KV_RANK))):
                    norm(l, n, rank, lat_rs[:, p, :])
                    project(l, 1, p)
                    split_lo(l, MIX0 + 2, p)
                up_projections(l)
                project(l, 2, 0)
                split_lo(l, MIX0 + 3, 0)
                for n in range(HEADS + 1):
                    if n < HEADS:
                        for i in range(QT):
                            if i == QT - 1 and n in SCORED:
                                project(l, *SCORED[n])
                            logits(l, n, i)
                    turned_in_slot(l, n, 0)
                    if n:
                        copy_pt(l, n - 1, 0)
                    if n >= 2:
                        outputs(l, n - 2)
                    if n + 1 < HEADS and ORDER[(n + 1) // G] in "AD":
                        mixer, h = head_out(n + 1)
                        earlier = 1 + h // 2 + (2 if mixer == "D" else 0)
                        dv.wait_ge(tab_in[(n + 1) % 2], l * 80 + 16 * (earlier + 1))
                    if n:
                        copy_pt(l, n - 1, 2)
                    for m, p in freed_panels(n):
                        split_lo(l, MIX0 + m + 1, p)
                    if n == 1:
                        gates_in(l)
                    if n == 2:
                        gates_out(l)
                    turned_in_slot(l, n, 1)
                    if n in LATER:
                        project(l, *LATER[n])
                outputs(l, HEADS - 1)
                outputs_lo(l, "D", 0)
                outputs_lo(l, "D", 1, bank[2])
                dv.sem_clear(s_full)
                for m in (6, 7):
                    for p in range(4):
                        panel_done(l, MIX0 + m, p)
                        d = 4 * (m - 6) + p
                        x_tile(l, bank[WO_BANK[p]], l * LAYER_X + 2 * KD + d, d, gain_at(l, 2, d), 1.0)
                        split_lo(l, MIX0 + m + 1, p)
                ffn(l, FFN2, 2, N_FFN2, False)
            norm(DEPTH, N_FFN1, D, rs[:])
            for d in range(KD):
                if d >= 2:
                    dv.wait_ge(z_turned, d - 1)
                g = 3 * DEPTH * KD + d
                dv.scalar_tensor_tensor(tmp[d % 2][:], x[:, d, :], gain[:, g:g + 1], rs[:], ALU.mult, ALU.mult
                                        ).then_inc(z_ready, 1)


def tables():
    t = np.arange(P)[:, None] + (T - P)
    dist = (t - np.arange(T)[None, :]).astype(np.int64)
    ok = dist >= 0
    f = np.float32
    out = [np.where(ok, 0.0, NEG)]
    inv = f(10000.0) ** (-np.arange(0, ROPE, 2, dtype=f) / f(ROPE))
    ang = inv[:, None] * np.arange(T, dtype=f)[None, :]
    cos, sin = np.cos(ang, dtype=f), np.sin(ang, dtype=f)
    out.append(np.tile(np.concatenate([cos, cos]), (G, 1)))
    out.append(np.tile(np.concatenate([-sin, sin]), (G, 1)))
    slopes = [2.0 ** (-8.0 * (i + 1) / (2 * G)) for i in range(2 * G)]
    count = (dist <= 128).astype(int) + (dist % 4 == 0) * (dist <= 512) + (dist % 16 == 0) * (dist <= 2048)
    log_count = np.log(np.maximum(count, 1).astype(np.float64))
    for s in slopes[1::2]:
        out.append(np.where(ok, -s * dist / SCALE, NEG))
    for s in slopes[0::2]:
        out.append(np.where(ok & (count > 0), (log_count - s * dist) / SCALE, NEG))
    return np.stack(out).astype(f)


_INS = ["x", "norm_ffn1", "ffn1_gate", "ffn1_up", "ffn1_down", "norm_mix", "w_in", "forget_bias", "mla_q_norm",
        "mla_kv_norm", "w_uq", "w_ukv", "w_out", "norm_ffn2", "ffn2_gate", "ffn2_up", "ffn2_down", "norm_final"]


def kernel(**inputs):
    import concourse.bacc as bacc
    from concourse.bass_utils import run_bass_kernel_spmd

    nc = bacc.Bacc("TRN2", target_bir_lowering=False, num_devices=1)
    sel_col = np.zeros((P, G), np.float32)
    for r in range(0, P, 32):
        sel_col[r:r + G] = np.eye(G)
    host = {n: np.ascontiguousarray(inputs[n]) for n in _INS}
    host |= {"c_ident": np.eye(P, dtype=np.float32), "c_sel": sel_col, "c_tables": tables()}
    args = {n: nc.dram_tensor(f"in_{n}", v.shape, F32, kind="ExternalInput").ap() for n, v in host.items()}
    out = nc.dram_tensor("out", (1, T, D), F32, kind="ExternalOutput").ap()
    build(nc, args, out)
    r = run_bass_kernel_spmd(nc, [{f"in_{n}": v for n, v in host.items()}], core_ids=[0])
    return r.results[0]["out"]
```

```python
from contextlib import ExitStack

import numpy as np

import concourse.bass as bass
from concourse import mybir

F32 = mybir.dt.float32
F32R = mybir.dt.float32r
ALU = mybir.AluOpType
ACT = mybir.ActivationFunctionType

P = 128
D = 1024
T = 512
DEPTH = 2
KD = D // P
QT = T // P
HD = 64
G = 4
HW = G * HD
FF = 256 * (-(-(8 * D) // (3 * 256)))
KF = FF // P
Q_RANK, KV_RANK, ROPE = D // 4, D // 8, HD // 2
EPS = 1e-6
NEG = -1e30
BIG = 3e38
SCALE = HD ** -0.5
EXP_LN = "natural_log_exp_and_others"
SCALE_MLA = (HD + ROPE) ** -0.5

GAINS = {"norm_ffn1": 0, "norm_final": DEPTH * KD, "norm_mix": (DEPTH + 1) * KD, "norm_ffn2": (2 * DEPTH + 1) * KD,
         "mla_q_norm": (3 * DEPTH + 1) * KD, "mla_kv_norm": (3 * DEPTH + 1) * KD + DEPTH * Q_RANK // P}
GAIN_ROWS = GAINS["mla_kv_norm"] + DEPTH
FIRST_SPLITS = {2: [0], KD - 1: [1, 2, 3]}
X_PARTS = 2
X_BANKS = (2, 3, 4, 5, 6)

AQ, AK, AV, BQ, BK, BV = (HW * i for i in range(6))
BF = 6 * HW
CQ = BF + G
CKV = CQ + Q_RANK
CKR = CKV + KV_RANK
DQ = CKR + ROPE
DK, DV = DQ + HW, DQ + 2 * HW

BLK = 256
GU_STEPS = FF // BLK
DN_K = (8, 8, KF - 16)
DN_PAIRS = D // BLK
DN_STEPS = 3 * DN_PAIRS // 2
FFN_STEPS = GU_STEPS + DN_STEPS
MIX_STEPS = 8
LAYER_STEPS = 2 * FFN_STEPS + MIX_STEPS
MIX0, FFN2 = FFN_STEPS, FFN_STEPS + MIX_STEPS

MIX_HEAD_OUTS = 14
MIX_OUTS = 30

U_FFN1, U_MIX, U_LQ, U_LKV = 0, 1, 2, 3
U_VT = {"C": 4, "A": 6, "B": 10, "D": 14}
U_OT = {"C": 8, "A": 12, "B": 16, "D": 18}
U_FFN2 = 20
LAYER_USES = 21
NORMS = 5
N_FFN1, N_MIX, N_LQ, N_LKV, N_FFN2 = range(NORMS)
LAYER_X = 3 * KD

ORDER = "CABD"
ROWS = {"A": 0, "B": 2, "C": 4, "D": 6}
HEADS = 4 * G

SCORED = {0: (2, 1), 1: (2, 2), 2: (2, 3), 4: (3, 1), 5: (3, 2), 6: (3, 3), 7: (4, 0), 8: (4, 1), 9: (4, 3),
          10: (5, 0), 11: (5, 2), 12: (5, 3)}
LATER = {3: (3, 0), 8: (4, 2), 10: (5, 1)}
EARLY_OUT = {13: 0, 14: 1}
LATE_SPLITS = (1, 4, 5, 6, 7, 9, 10, 11)
SLOT_VT = {(0, 0): "C", (1, 1): "C", (3, 0): "A", (3, 1): "A", (9, 0): "B", (9, 1): "B", (13, 0): "D", (13, 1): "D"}
SLOT_OT = {(6, 0): "C", (6, 1): "C", (10, 0): "A", (10, 1): "A", (14, 0): "B", (14, 1): "B"}
DEST = {(1, 0): "qA0", (1, 1): "qA1", (2, 0): "kA0", (2, 1): "kA1", (2, 2): "vA0", (2, 3): "vA1",
        (3, 0): "qB0", (3, 1): "qB1", (3, 2): "kB0", (3, 3): "kB1", (4, 0): "vB0", (4, 1): "vB1",
        (4, 2): "qD0", (4, 3): "qD1", (5, 0): "kD0", (5, 1): "kD1", (5, 2): "vD0", (5, 3): "vD1"}
MIX_COLS = {(1, 0): AQ, (2, 0): AK, (2, 1): AV, (3, 0): BQ, (3, 1): BK, (4, 0): BV, (4, 1): DQ,
            (5, 0): DK, (5, 1): DV}

TRI = [P * i * (i + 1) // 2 for i in range(QT + 1)]
TRT = [0, T, 2 * T, 2 * T - P]


def mix_out(s, p, o=0):
    base = {0: 0, 1: 4}.get(s, 14 + 4 * (s - 2))
    if s == 1:
        return base + {0: 0, 1: 1, 2: 2, 3: 6}[p] + o
    return base + p


def gain_col(l, g, d):
    l, name = (l + 1, "norm_ffn1") if g == 3 else (l, ("norm_ffn1", "norm_mix", "norm_ffn2")[g])
    return bass.ds(l * KD + (GAINS[name] + d), 1)


def out_bank(j):
    if j == MIX_HEAD_OUTS:
        return 5, -1
    return (j % 4, j - 4) if j < MIX_HEAD_OUTS else (j % 2, j - 2)


def split_operand(m, p):
    names = [x + y + z for x in "ABD" for y in "qk" for z in "01"]
    name = DEST[m, p]
    return names.index(name[1] + name[0] + name[2]) if name[0] != "v" else None


def operands_in(n):
    last = (5, 1)
    return [last] * (n == 3 * G) + [s for s in freed_panels(n) if split_operand(*s) is not None and s != last]


def freed_panels(n):
    return [slots[n - 1] for slots in (SCORED, LATER) if n - 1 in slots]


def k_tiles(mixers):
    return [ROWS[m] + j for m in mixers for j in range(2)]


def head_out(n):
    return ORDER[n // G], n % G


def raw_dmas(slot, s):
    return s + 1 + (slot == 1) * (s >= MIX0) + (s >= MIX0 + 1)


def build(nc, a, out):
    ctx = ExitStack()
    with ctx:
        def sb(name, shape, dt=F32):
            return ctx.enter_context(nc.sbuf_tensor(name, shape, dt))

        def sem(name):
            return ctx.enter_context(nc.semaphore(name))

        x = sb("x", [P, KD, T])
        xg_hi = sb("xg_hi", [P, KD, T], F32R)
        xg_lo = sb("xg_lo", [P, KD, T], F32R)
        raw = [sb(f"raw{r}", [P, KD * BLK]) for r in range(2)]
        hi = [sb(f"panel_hi{p}", [P, 8 * P], F32R) for p in range(4)]
        lo = [sb(f"panel_lo{p}", [P, 8 * P], F32R) for p in range(4)]
        rs = sb("rs", [P, T])
        tmp = [sb(f"tmp{j}", [P, T]) for j in range(2)]
        act = [sb(f"act{j}", [P, T]) for j in range(2)]
        sel = sb("sel", [P, G, P], F32R)
        dec = sb("dec", [P, T], F32R)
        ident_r = dec[:, 0:P]
        tab = [sb(f"tab{j}", [P, T]) for j in range(2)]
        causal = sb("causal", [P, T])
        ident = sb("ident", [P, P])
        ones = sb("ones", [P, P])
        gain = sb("gain", [P, GAIN_ROWS])
        neg_max = sb("neg_max", [P, 2, QT])
        row_sum = sb("row_sum", [P, 4, QT])
        inv_sum = sb("inv_sum", [P, 2, QT])
        fbias = sb("fbias", [P, DEPTH])
        gate = sb("gate", [P, T])
        sel_col = sb("sel_col", [P, G])

        start = -(-nc.sbuf_base // 32) * 32
        sb("region", [P, 2 * KF * T])

        def at(name, offset, shape, dt=F32):
            return nc.alloc_sbuf_tensor_at(name, shape, dt, offset=start + 4 * offset)

        x_rows = at("x_rows", 0, [P, QT, D])
        y_rows = at("y_rows", 0, [P, QT, D])
        gain_rows = at("gain_rows", QT * D, [P, P])
        a_hi = at("a_hi", 0, [P, KF, T], F32R)
        a_lo = at("a_lo", KF * T, [P, KF, T], F32R)
        mix_hi = at("mix_hi", 0, [P, KD, T], F32R)
        mix_lo = at("mix_lo", KD * T, [P, KD, T], F32R)
        lat = at("lat", 0, [P, 3, T])
        lat_hi = at("lat_hi", 3 * T, [P, 3, T], F32R)
        lat_lo = at("lat_lo", 6 * T, [P, 3, T], F32R)
        lat_sq = at("lat_sq", 9 * T, [P, 3, T])
        lat_rs = at("lat_rs", 12 * T, [P, 2, T])
        rot = at("rot", 14 * T, [P, 2, T])
        o1 = 2 * KD * T
        q1 = at("q1", o1, [P, G, T])
        k1 = at("k1", o1 + 4 * T, [P, G, T])
        v1 = at("v1", o1 + 8 * T, [P, QT, HW])
        v2 = at("v2", o1 + 14 * T, [P, QT, HW])
        o2 = o1 + 16 * T
        prob = [at(f"prob{j}", o2 + j * TRI[QT], [P, TRI[QT]]) for j in range(2)]
        probT = [at(f"probT{j}", o2 + (2 + j) * TRI[QT], [P, TRI[QT]]) for j in range(2)]
        o_rows = at("o_rows", o2 + 4 * TRI[QT], [P, QT, HW])
        values = {"C": v1, "B": v1, "A": v2, "D": v2}
        split_q = {m: at(f"split_q{m}", place_, [P, G, T], F32R)
                   for m, place_ in (("A", o1 + 10 * T), ("B", o1), ("D", o1 + 10 * T))}
        keys_at = {"A": (2 * T, (KD + 2) * T), "B": (o1 + 4 * T, o1 + 6 * T), "D": (2 * T, o1)}
        keys_hi = {m: [at(f"keys_hi{m}{j}", keys_at[m][j], [P, 2, T], F32R) for j in range(2)] for m in keys_at}
        keys_lo = {m: at(f"keys_lo{m}", row * T, [P, 2, T], F32R) for m, row in (("A", 6), ("B", KD + 6), ("D", 6))}
        k_misc = at("k_misc", o1 + 14 * T, [P, T])
        k_rot = at("k_rot", o1 + 15 * T, [P, T])

        bank = [ctx.enter_context(nc.psum_tensor(f"bank{b}", [P, T], F32)) for b in range(8)]
        S_BANK, PT_EVEN, PT_ODD, O_BANK, SMALL = (2, 3), bank[4], bank[5], bank[6], bank[7]
        LAST_SUMS = SMALL[:, T - P:T - P + QT]
        LKV_BANK = bank[4]
        WO_BANK = (0, 1, 3, 4)

        LAT_V = (tmp[0][:], lat_sq[:, 1, :])
        LAT_GUESS = (tmp[1][:], lat_sq[:, 2, :])
        gate_z = at("gate_z", KD * T, [P, T])[0:G, :]

        gains_in = sem("gains_in")
        gain_ready = sem("gain_ready")
        consts_in = sem("consts_in")
        x_in = [sem(f"x_in{h}") for h in range(X_PARTS)]
        setup_done = sem("setup_done")
        gain_full = sem("gain_full")
        turned = sem("turned")
        raw_in = [sem(f"raw_in{r}") for r in range(2)]
        hi_ready = sem("hi_ready")
        lo_ready = sem("lo_ready")
        panel_used = sem("panel_used")
        out_free = sem("out_free")
        up_full = sem("up_full")
        x_ready = sem("x_ready")
        xg_hi_ready = sem("xg_hi_ready")
        xg_lo_ready = sem("xg_lo_ready")
        sq_ready = sem("sq_ready")
        sq_summed = sem("sq_summed")
        small_full = sem("small_full")
        small_free = sem("small_free")
        ln_done = sem("ln_done")
        guess = sem("guess")
        newton = sem("newton")
        rs_ready = sem("rs_ready")
        gated = sem("gated")
        silu_ready = sem("silu_ready")
        silu_scaled = sem("silu_scaled")
        a_ready = sem("a_ready")
        a_hi_ready = sem("a_hi_ready")
        a_lo_ready = sem("a_lo_ready")
        lat_sq_ready = sem("lat_sq_ready")
        lat_hi_ready = sem("lat_hi_ready")
        lat_lo_ready = sem("lat_lo_ready")
        lat_summed = sem("lat_summed")
        rope_in = sem("rope_in")
        rope_mul = sem("rope_mul")
        rope_done = sem("rope_done")
        ident_ready = sem("ident_ready")
        rope_keys = sem("rope_keys")
        tab_in = [sem(f"tab_in{j}") for j in range(2)]
        gate_step = sem("gate_step")
        gate_exp = sem("gate_exp")
        operand_hi = sem("operand_hi")
        operand_lo = sem("operand_lo")
        s_full = sem("s_full")
        logits_ready = sem("logits_ready")
        exp_ready = sem("exp_ready")
        pt_full = sem("pt_full")
        pt_even = sem("pt_even")
        pt_odd = sem("pt_odd")
        o_full = sem("o_full")
        inv_ready = sem("inv_ready")
        o_ready = sem("o_ready")
        mix_hi_ready = sem("mix_hi_ready")
        y_even = sem("y_even")
        y_odd = sem("y_odd")
        y_out = sem("y_out")

        block = ctx.enter_context(nc.Block())

        def rawv(r, k, lo_col, n):
            return raw[r][:, 0:k * BLK].rearrange("p (k c) -> p k c", c=BLK)[:, :, lo_col:lo_col + n]

        def pan(buf, k, n=P):
            return buf[:, 0:k * n].rearrange("p (k c) -> p k c", c=n)

        def pieces(s, p):
            s %= LAYER_STEPS
            r, half = p // 2, P * (p % 2)
            if MIX0 <= s < FFN2:
                m = s - MIX0
                if (m, p) == (0, 3):
                    v, H = KV_RANK, ROPE // 2
                    return [((0, ROPE), rawv(r, KD, v, ROPE)), ((ROPE, ROPE + H), rawv(r, KD, v + H, H)),
                            ((ROPE + H, 2 * ROPE), rawv(r, KD, v, H)),
                            ((2 * ROPE, 2 * ROPE + G), rawv(r, KD, v + ROPE, G))]
                if m == 1 and p >= 2:
                    kq, nq, nk = Q_RANK // P, G * (HD + ROPE), G * 2 * HD
                    if p == 3:
                        w = raw[1][:, kq * nq:kq * nq + nk].rearrange("p (k h c) -> p k h c", k=1, h=G)
                        return [(("h", 1, 0, HD, 0, HD), w[:, :, :, 0:HD]),
                                (("h", 1, HW, HD, 0, HD), w[:, :, :, HD:2 * HD])]
                    w = raw[1][:, 0:kq * nq].rearrange("p (k h c) -> p k h c", k=kq, h=G)
                    H = ROPE // 2
                    return [(("h", kq, 0, HD, 0, HD), w[:, :, :, 0:HD]),
                            (("h", kq, HW, ROPE, 0, ROPE), w[:, :, :, HD:HD + ROPE]),
                            (("h", kq, HW + G * ROPE, ROPE, 0, H), w[:, :, :, HD + H:HD + ROPE]),
                            (("h", kq, HW + G * ROPE, ROPE, H, ROPE), w[:, :, :, HD:HD + H])]
                return [((0, P), rawv(r, KD, half, P))]
            d = s - GU_STEPS if s < MIX0 else s - FFN2 - GU_STEPS
            k = KD if d < 0 else DN_K[(2 * d + r) % 3]
            return [((0, P, k), rawv(r, k, half, P))]

        def place(buf, how, k=KD):
            if how[0] == "h":
                _, kq, c0, w, j0, j1 = how
                full = buf[:, 0:kq * 2 * HW].rearrange("p (k c) -> p k c", k=kq)[:, :, c0:c0 + G * w]
                return full.rearrange("p k (h c) -> p k h c", h=G)[:, :, :, j0:j1]
            k = how[2] if len(how) == 3 else k
            return pan(buf, k)[:, :, how[0]:how[1]]

        def each_piece(how, dst, src):
            if how[0] == "h":
                return [(dst(how)[:, k], src[:, k]) for k in range(how[1])]
            return [(dst(how), src)]

        @block.sync
        def _(sp):
            for h in range(X_PARTS):
                c = slice(h * D // X_PARTS, (h + 1) * D // X_PARTS)
                sp.dma_start(x_rows[:, :, c], a["x"].rearrange("o (q p) d -> p (o q) d", p=P)[:, :, c]
                             ).then_inc(x_in[h], 16)
                if h == 0:
                    sp.dma_start(ident[:], a["c_ident"]).then_inc(gains_in, 16)
                    for g, row in GAINS.items():
                        src = a[g].rearrange("(k p) -> k p", p=P) if g == "norm_final" else \
                            a[g].rearrange("l (k p) -> (l k) p", p=P)
                        sp.dma_start(gain_rows[row:row + src.shape[0], :], src).then_inc(gains_in, 16)

            def block_in(l, step, r, src, dst):
                sp.wait_ge(lo_ready, l * (4 * LAYER_STEPS) + step * 4 + 2 * r + 2)
                for d, s in zip(dst, src):
                    sp.dma_start(d, s).then_inc(raw_in[r], 16)

            def cols(w, l, c, n=BLK):
                tiles = w.shape[1] // P
                at_ = slice(c, c + n) if isinstance(c, int) else bass.ds(c, n)
                return w.rearrange("l (k p) n -> p (l k) n", p=P)[:, bass.ds(l * tiles, tiles), at_]

            def gate_up_in(l, s0, name, i):
                for r, w in enumerate(("gate", "up")):
                    block_in(l, s0 + i, r, [cols(a[f"{name}_{w}"], l, i * BLK)], [rawv(r, KD, 0, BLK)])

            def ffn_in(l, s0, name):
                if s0:
                    gate_up_in(l, s0, name, 0)
                with sp.Fori(1, GU_STEPS) as i:
                    gate_up_in(l, s0, name, i)
                for b in range(3 * DN_PAIRS):
                    pair, third = b // 3, b % 3
                    src = cols(a[f"{name}_down"], l, pair * BLK)[:, 8 * third:8 * third + DN_K[third], :]
                    block_in(l, s0 + GU_STEPS + b // 2, b % 2, [src], [rawv(b % 2, DN_K[third], 0, BLK)])

            def layer_in(l):
                ffn_in(l, 0, "ffn1")
                block_in(l, MIX0, 0, [cols(a["w_in"], l, CQ)], [rawv(0, KD, 0, BLK)])
                block_in(l, MIX0, 1, [cols(a["w_in"], l, CKV, KV_RANK + ROPE), cols(a["w_in"], l, BF, G)],
                         [rawv(1, KD, 0, KV_RANK + ROPE), rawv(1, KD, KV_RANK + ROPE, G)])
                block_in(l, MIX0 + 1, 0, [cols(a["w_in"], l, AQ)[:, 1:KD], cols(a["w_in"], l, AQ)[:, 0:1]],
                         [rawv(0, KD, 0, BLK)[:, 1:KD], rawv(0, KD, 0, BLK)[:, 0:1]])
                nq, nk = G * (HD + ROPE), G * 2 * HD
                block_in(l, MIX0 + 1, 1,
                         [a["w_uq"][bass.ds(l, 1)].rearrange("o (k p) n -> p (o k) n", p=P),
                          a["w_ukv"][bass.ds(l, 1)].rearrange("o p n -> p (o n)")],
                         [raw[1][:, 0:2 * nq].rearrange("p (k n) -> p k n", k=2),
                          raw[1][:, 2 * nq:2 * nq + nk]])
                for m in range(2, 6):
                    for r in range(2):
                        block_in(l, MIX0 + m, r, [cols(a["w_in"], l, MIX_COLS[m, r])], [rawv(r, KD, 0, BLK)])
                for m in range(6, 8):
                    for r in range(2):
                        block_in(l, MIX0 + m, r, [cols(a["w_out"], l, (2 * (m - 6) + r) * BLK)],
                                 [rawv(r, KD, 0, BLK)])
                ffn_in(l, FFN2, "ffn2")

            gate_up_in(0, 0, "ffn1", 0)
            with sp.Fori(0, DEPTH - 1) as l:
                layer_in(l)
                gate_up_in(l + 1, 0, "ffn1", 0)
            layer_in(DEPTH - 1)
            for r in range(2):
                sp.wait_ge(lo_ready, DEPTH * (4 * LAYER_STEPS) + 2 * r + 2)
                sp.sem_inc(raw_in[r], 16)
            for q in range(QT):
                sp.wait_ge(y_even, q + 1)
                sp.wait_ge(y_odd, q + 1)
                sp.dma_start(out[0, P * q:P * (q + 1), :], y_rows[:, q, :]).then_inc(y_out, 16)
            sp.wait_ge(y_out, 16 * QT)

        @block.tensor
        def _(pe):
            pe.wait_ge(gains_in, 16 * (1 + len(GAINS)))
            pe.transpose(SMALL[:, 0:GAIN_ROWS], gain_rows[0:GAIN_ROWS, :], ident[0:GAIN_ROWS, 0:GAIN_ROWS]
                         ).then_inc(gain_full, 1)
            for d in range(KD):
                if d % (KD // X_PARTS) == 0:
                    pe.wait_ge(x_in[d // (KD // X_PARTS)], 16)
                if d >= len(X_BANKS):
                    pe.wait_ge(x_ready, d - len(X_BANKS) + 1)
                for q in range(QT):
                    last = pe.transpose(bank[X_BANKS[d % len(X_BANKS)]][:, P * q:P * (q + 1)],
                                        x_rows[:, q, P * d:P * (d + 1)], ident[:])
                last.then_inc(turned, 1)

            def panel_ready(l, step, p):
                pe.wait_ge(lo_ready, l * (4 * LAYER_STEPS) + step * 4 + p + 5)

            def products(dst, p, k, rhs_hi, rhs_lo, first, last, col=0, n=P, width=P, k0=0, kp=0):
                w_hi, w_lo = pan(hi[p], kp + k, width), pan(lo[p], kp + k, width)
                for j in range(k):
                    for t, (w, v) in enumerate(((w_hi, rhs_hi), (w_hi, rhs_lo), (w_lo, rhs_hi))):
                        mm = pe.matmul(dst, w[:, kp + j, col:col + n], v[:, k0 + j, :],
                                       start=first and j == 0 and t == 0, stop=last and j == k - 1 and t == 2)
                return mm

            def small_use(l, u):
                if u:
                    pe.wait_ge(small_free, l * LAYER_USES + u)

            def sum_squares(l, u, src, dst=SMALL):
                if dst is SMALL:
                    small_use(l, u)
                pe.matmul(dst[:], ones[:], src, start=True, stop=True).then_inc(small_full, 1)

            def first_products(l, nth, dst, p):
                if nth == 2:
                    pe.wait_ge(x_ready, l * LAYER_X + 2 * KD + 5)
                for j in range(KD):
                    pe.wait_ge(xg_lo_ready, l * LAYER_X + KD * nth + j + 1)
                    mm = products(dst, p, 1, xg_hi, xg_lo, j == 0, j == KD - 1, k0=j, kp=j)
                return mm

            def ffn(l, s0, nth, use):
                def gate_up(i, first=False):
                    for p in range(4):
                        panel_ready(l, s0 + i, p)
                        if not first:
                            pe.wait_ge(gated if p < 2 else a_ready,
                                       l * (2 * KF) + (KF if s0 else 0) + i * 2 + p % 2 - 1)
                        if first and p == 0:
                            mm = first_products(l, nth, bank[p][:], p)
                        else:
                            mm = products(bank[p][:], p, KD, xg_hi, xg_lo, True, True)
                        mm.then_inc(panel_used, 1)
                        if first and p == 0:
                            pe.wait_ge(sq_summed, (l * 3 + nth + 1) * (KD - 1))
                            sum_squares(l, use, act[0][:])

                gate_up(0, first=True)
                with pe.Fori(1, GU_STEPS) as i:
                    gate_up(i)
                for b in range(3 * DN_PAIRS):
                    pair, third = b // 3, b % 3
                    if pair == 0:
                        pe.wait_ge(a_lo_ready, l * (2 * KF) + (KF if s0 else 0) + 8 * third + DN_K[third])
                    for h in range(2):
                        p = 2 * (b % 2) + h
                        panel_ready(l, s0 + GU_STEPS + b // 2, p)
                        if third == 0 and pair:
                            pe.wait_ge(x_ready, l * LAYER_X + KD * (nth + 1) + 2 * pair + h - 1)
                        products(bank[4 + h][:], p, DN_K[third], a_hi, a_lo, third == 0, third == 2,
                                 k0=8 * third).then_inc(panel_used, 1)

            def project(l, m, p, ks=range(KD)):
                j = mix_out(m, p)
                b, former = out_bank(j)
                n = 2 * ROPE + G if (m, p) == (0, 3) else P
                if ks[0] == 0:
                    panel_ready(l, MIX0 + m, p)
                    if former >= 0:
                        pe.wait_ge(out_free, l * MIX_OUTS + former + 1)
                mm = products(bank[b][0:n, :], p, len(ks), xg_hi, xg_lo, ks[0] == 0, ks[-1] == KD - 1, n=n,
                              k0=ks[0], kp=ks[0])
                if ks[-1] == KD - 1:
                    mm.then_inc(panel_used, 1)

            def project_out(l, d, ks):
                p = d % 4
                if ks[0] == 0:
                    panel_ready(l, MIX0 + 6 + d // 4, p)
                    if d < 2:
                        pe.wait_ge(out_free, l * MIX_OUTS + MIX_OUTS - 1 + d)
                    if d >= 4:
                        pe.wait_ge(x_ready, l * LAYER_X + 2 * KD + d - 3)
                for k in ks:
                    mm = products(bank[WO_BANK[p]][:], p, 1, mix_hi, mix_lo, k == 0, k == KD - 1, k0=k, kp=k)
                if ks[-1] == KD - 1:
                    mm.then_inc(panel_used, 1)

            def up_project(l, p):
                panel_ready(l, MIX0 + 1, p)
                k0, k = (0, Q_RANK // P) if p == 2 else (Q_RANK // P, 1)
                pe.wait_ge(lat_lo_ready, l * 3 + k0 + k)
                for o in range(4):
                    b, former = out_bank(mix_out(1, p, o))
                    pe.wait_ge(out_free, l * MIX_OUTS + former + 1)
                    mm = products(bank[b][:], p, k, lat_hi, lat_lo, True, True, col=P * o, width=2 * HW, k0=k0)
                    mm.then_inc(panel_used if o == 3 else up_full, 1)

            def queries_ready(l, n):
                mixer, h = head_out(n)
                if mixer == "C":
                    pe.wait_ge(rope_keys, l + 1)
                    pe.wait_ge(rope_done, l * 5 + 5)
                    pe.wait_ge(out_free, l * MIX_OUTS + mix_out(1, 3, 1) + 1)
                else:
                    keys = next(sp_ for sp_, d in DEST.items() if d == f"k{mixer}{h // 2}")
                    pe.wait_ge(operand_lo, l * (6 * G) + 2 * split_operand(*keys) + 2)
                if n == 2 * G:
                    pe.wait_ge(setup_done, 8)
                    pe.wait_ge(gate_step, l * 9 + 9)

            def scores(l, n, i):
                mixer, h = head_out(n)
                own = slice(HD * (h % 2), HD * (h % 2 + 1))
                e = 4 * n + i
                if i == 0:
                    queries_ready(l, n)
                if e >= 2:
                    pe.wait_ge(logits_ready, l * (4 * HEADS) + e - 1)
                w = P * (i + 1)
                dst = bank[S_BANK[i % 2]][:, 0:w]
                if mixer == "C":
                    pe.matmul(dst, q1[0:HD + ROPE, h, P * i:P * (i + 1)], k1[0:HD + ROPE, h, 0:w],
                              start=True, stop=True).then_inc(s_full, 1)
                    return
                if mixer == "B":
                    r = slice(own.start, own.start + 36)
                    pe.matmul(dst, sel[r, h, :], dec[r, 0:w], start=True, stop=False)
                pe.matmul(dst, split_q[mixer][:, h, P * i:P * (i + 1)], keys_hi[mixer][h // 2][:, h % 2, 0:w],
                          start=mixer != "B", stop=False)
                pe.matmul(dst, split_q[mixer][own, h, P * i:P * (i + 1)], keys_lo[mixer][own, h // 2, 0:w],
                          start=False, stop=True).then_inc(s_full, 1)

            def turn_probs(l, n, kts):
                for kt in kts:
                    for i in range(kt, QT):
                        dst, c = (PT_ODD, TRT[kt] - TRT[1] - P * kt) if kt % 2 else (PT_EVEN, 0)
                        last = pe.transpose(dst[:, c + P * i:c + P * (i + 1)],
                                            prob[n % 2][:, TRI[i] + P * kt:TRI[i] + P * (kt + 1)], ident[:])
                last.then_inc(pt_full, 1)

            def weigh_values(l, n):
                mixer, h = head_out(n)
                v = values[mixer]
                pe.wait_ge(pt_even, l * (2 * HEADS) + 2 * n + 2)
                pe.wait_ge(pt_odd, l * HEADS + n + 1)
                if h == 0:
                    pe.wait_ge(small_free, l * LAYER_USES + U_VT[mixer] + 2)
                if n:
                    pe.wait_ge(o_ready, l * HEADS + n)
                for i in range(QT):
                    for kt in range(i + 1):
                        c = TRT[kt] + P * (i - kt)
                        last = pe.matmul(O_BANK[:, HD * i:HD * (i + 1)], probT[n % 2][:, c:c + P],
                                         v[:, kt, HD * h:HD * (h + 1)], start=kt == 0, stop=kt == i)
                last.then_inc(o_full, 1)

            def turn_values(l, mixer, pair):
                if mixer == "C":
                    done = mix_out(1, 3, 2 + pair)
                else:
                    done = mix_out(*next(k_ for k_, d in DEST.items() if d == f"v{mixer}{pair}"))
                pe.wait_ge(out_free, l * MIX_OUTS + done + 1)
                small_use(l, U_VT[mixer] + pair)
                for q in range(QT):
                    last = pe.transpose(SMALL[:, P * q:P * (q + 1)], tmp[pair][:, P * q:P * (q + 1)], ident[:])
                last.then_inc(small_full, 1)

            def turn_outputs(l, mixer, pair, dst=SMALL):
                pe.wait_ge(o_ready, l * HEADS + G * (ORDER.index(mixer) + 1))
                if dst is SMALL:
                    small_use(l, U_OT[mixer] + pair)
                for q in range(QT):
                    last = pe.transpose(dst[:, P * q:P * (q + 1)],
                                        o_rows[:, q, P * pair:P * (pair + 1)], ident[:])
                last.then_inc(small_full, 1)

            def turn(l, n, pair):
                if (n, pair) in SLOT_VT:
                    turn_values(l, SLOT_VT[n, pair], pair)
                if (n, pair) in SLOT_OT:
                    turn_outputs(l, SLOT_OT[n, pair], pair)

            def turn_first(l, n):
                pe.wait_ge(exp_ready, l * (4 * HEADS) + 4 * n + 4)
                if n:
                    pe.wait_ge(pt_even, l * (2 * HEADS) + 2 * n)
                turn_probs(l, n, [0])

            def turn_odd(l, n):
                if n:
                    pe.wait_ge(pt_odd, l * HEADS + n)
                turn_probs(l, n, [1, 3])

            def turn_last(l, n):
                pe.wait_ge(pt_even, l * (2 * HEADS) + 2 * n + 1)
                turn_probs(l, n, [2])

            with pe.Fori(0, DEPTH) as l:
                ffn(l, 0, 0, U_FFN1)
                panel_ready(l, MIX0, 0)
                first_products(l, 1, bank[0][:], 0).then_inc(panel_used, 1)
                pe.wait_ge(sq_summed, (l * 3 + 2) * (KD - 1))
                sum_squares(l, U_MIX, act[0][:])
                for p in (1, 2, 3):
                    project(l, 0, p)
                pe.wait_ge(lat_summed, l + 1)
                sum_squares(l, U_LQ, lat_sq[:, 0, :])
                pe.wait_ge(lat_sq_ready, l * 3 + 3)
                sum_squares(l, U_LKV, lat_sq[:, 2, :], LKV_BANK)
                project(l, 1, 0)
                project(l, 1, 1)
                up_project(l, 2)
                up_project(l, 3)
                project(l, 2, 0)
                for n in range(HEADS):
                    if n in SCORED:
                        for i in range(QT):
                            project(l, *SCORED[n], ks=range(2 * i, 2 * i + 2))
                            scores(l, n, i)
                        turn(l, n, 0)
                        if n:
                            turn_first(l, n - 1)
                            turn_odd(l, n - 1)
                    else:
                        scores(l, n, 0)
                        scores(l, n, 1)
                        if n in EARLY_OUT:
                            project_out(l, EARLY_OUT[n], k_tiles("A"))
                        turn_first(l, n - 1)
                        scores(l, n, 2)
                        turn_odd(l, n - 1)
                        scores(l, n, 3)
                        turn(l, n, 0)
                    if n >= 2:
                        weigh_values(l, n - 2)
                    if n in EARLY_OUT:
                        project_out(l, EARLY_OUT[n], k_tiles("C"))
                    turn(l, n, 1)
                    if n:
                        turn_last(l, n - 1)
                    if n in LATER:
                        project(l, *LATER[n])
                project_out(l, 0, k_tiles("B"))
                turn_first(l, HEADS - 1)
                turn_odd(l, HEADS - 1)
                weigh_values(l, HEADS - 2)
                turn_last(l, HEADS - 1)
                project_out(l, 2, k_tiles("ABC"))
                weigh_values(l, HEADS - 1)
                project_out(l, 1, k_tiles("B"))
                turn_outputs(l, "D", 0)
                turn_outputs(l, "D", 1, bank[2])
                project_out(l, 3, k_tiles("ABC"))
                pe.wait_ge(small_free, l * LAYER_USES + U_OT["D"] + 2)
                for d in range(4):
                    project_out(l, d, k_tiles("D"))
                for d in range(4, KD):
                    project_out(l, d, k_tiles("ABCD"))
                ffn(l, FFN2, 2, U_FFN2)
            base = 3 * DEPTH * KD
            pe.wait_ge(ident_ready, DEPTH)
            pe.wait_ge(xg_lo_ready, base + KD - 1)

            def turn_x(q, d):
                dst = bank[2 * q + d // (KD // 2)][:, P * (d % (KD // 2)):][:, 0:P]
                pe.matmul(dst, xg_hi[:, d, P * q:P * (q + 1)], ident_r, start=True, stop=False)
                return pe.matmul(dst, xg_lo[:, d, P * q:P * (q + 1)], ident_r, start=False, stop=True)

            for q in (0, 1, 3, 2):
                if q == 2:
                    pe.wait_ge(x_ready, base + KD)
                for d in range(KD - 1):
                    turn_x(q, d)
            pe.wait_ge(sq_summed, (3 * DEPTH + 1) * (KD - 1))
            for q in range(QT):
                last = pe.matmul(LAST_SUMS[:, q:q + 1], act[0][:, P * q:P * (q + 1)], ones[:, 0:1],
                                 start=True, stop=True)
            last.then_inc(small_full, 1)
            pe.wait_ge(xg_lo_ready, base + KD)
            for q in range(QT):
                if q == QT - 1:
                    pe.wait_ge(small_free, DEPTH * LAYER_USES + 1)
                turn_x(q, KD - 1).then_inc(turned, 1)

        @block.scalar
        def _(sc):
            def split_hi(l, s, p, step=None):
                step = s if step is None else step
                sc.wait_ge(panel_used, l * (4 * LAYER_STEPS) + step * 4 + p + 1)
                r = p // 2
                sc.wait_ge(raw_in[r], l * (16 * raw_dmas(r, LAYER_STEPS - 1)) + step * 16
                           + 16 * (raw_dmas(r, s) - s))
                for how, src in pieces(s, p):
                    for d, v in each_piece(how, lambda h_: place(hi[p], h_), src):
                        last = sc.activation(d, v, ACT.Copy)
                last.then_inc(hi_ready, 1)

            def x_tile(m, d, g):
                sc.wait_ge(x_ready, m * KD + d + 1)
                sc.activation(xg_hi[:, d, :], x[:, d, :], ACT.Copy, scale=gain[:, g]).then_inc(xg_hi_ready, 1)
                if d >= 3:
                    sc.wait_ge(sq_summed, m * (KD - 1) + d - 2)
                sc.activation((tmp[d % 2] if d else act[0])[:], x[:, d, :], ACT.Square).then_inc(sq_ready, 1)

            def norm_guess(l, n):
                c = l * NORMS + n
                use = {N_FFN1: U_FFN1, N_MIX: U_MIX, N_FFN2: U_FFN2}[n]
                sc.preload_act_table_set(EXP_LN)
                sc.wait_ge(small_free, l * LAYER_USES + use + 1)
                sc.activation(tmp[1][:], tmp[0][:], ACT.Ln).then_inc(ln_done, 1)
                sc.wait_ge(ln_done, c + 1)
                sc.activation(tmp[1][:], tmp[1][:], ACT.Exp, scale=-0.5).then_inc(guess, 1)

            def latent_guesses(l):
                for j in range(2):
                    v, g = LAT_V[j], LAT_GUESS[j]
                    sc.wait_ge(small_free, l * LAYER_USES + (U_LQ, U_LKV)[j] + 1)
                    sc.activation(g[:], v[:], ACT.Ln).then_inc(ln_done, 1)
                for j in range(2):
                    sc.wait_ge(ln_done, l * NORMS + (N_LQ, N_LKV)[j] + 1)
                    sc.activation(LAT_GUESS[j][:], LAT_GUESS[j][:], ACT.Exp, scale=-0.5).then_inc(guess, 1)

            def ffn(l, s0, nth, nrm):
                def gate_up(i, following, step, first=False):
                    for p in range(4):
                        split_hi(l, following, p, step)
                        f = l * (2 * KF) + (KF if s0 else 0) + i * 2 + p % 2 + 1
                        if first and p == 0:
                            norm_guess(l, nrm)
                        if p < 2:
                            sc.wait_ge(gated, f)
                            sc.activation(tmp[p][:], tmp[p][:], ACT.Silu).then_inc(silu_ready, 1)
                        else:
                            sc.wait_ge(a_ready, f)
                            sc.activation(a_hi[:, bass.ds(i * 2 + p - 2, 1), :],
                                          act[p - 2][:].unsqueeze(1), ACT.Copy).then_inc(a_hi_ready, 1)

                gate_up(0, s0, s0 + 1, first=True)
                with sc.Fori(1, GU_STEPS - 1) as i:
                    gate_up(i, s0, s0 + i + 1)
                gate_up(GU_STEPS - 1, s0 + GU_STEPS, s0 + GU_STEPS)
                for b in range(3 * DN_PAIRS):
                    s = s0 + GU_STEPS + b // 2
                    for h in range(2):
                        split_hi(l, s + 1, 2 * (b % 2) + h)
                        if b % 3 == 2:
                            d = 2 * (b // 3) + h
                            x_tile(l * 3 + nth + 1, d, gain_at(l, nth + 1, d))

            def gain_at(l, g, d):
                return gain_col(l, g, d)

            def copy_pt(l, n):
                sc.wait_ge(pt_full, l * (3 * HEADS) + 3 * n + 2)
                if n >= 2:
                    sc.wait_ge(o_full, l * HEADS + n - 1)
                sc.activation(probT[n % 2][:, TRT[1]:TRT[1] + T], PT_ODD[:], ACT.Copy).then_inc(pt_odd, 1)

            def queries_keys_hi(l, m, p):
                kind, mixer, pair = DEST[m, p][0], DEST[m, p][1], int(DEST[m, p][2])
                sc.wait_ge(out_free, l * MIX_OUTS + mix_out(m, p) + 1)
                for e in range(2):
                    own = slice(HD * e, HD * (e + 1))
                    if kind == "q":
                        last = sc.activation(split_q[mixer][own, 2 * pair + e, :], act[pair][own, :], ACT.Copy)
                    else:
                        for half in (slice(0, HD), slice(HD, P)):
                            last = sc.activation(keys_hi[mixer][pair][half, e, :], act[pair][own, :], ACT.Copy)
                last.then_inc(operand_hi, 1)

            def outputs_hi(l, mixer, pair, src=SMALL):
                sc.wait_ge(small_full, l * LAYER_USES + U_OT[mixer] + pair + 1)
                sc.activation(mix_hi[:, ROWS[mixer] + pair, :], src[:], ACT.Copy).then_inc(mix_hi_ready, 1)

            def table_in(which, j):
                sc.dma_start(tab[j][:], a["c_tables"][which]).then_inc(tab_in[j], 16)

            def latent(l, j):
                sc.wait_ge(out_free, l * MIX_OUTS + j + 1)
                sc.activation(lat_sq[:, j, :], lat[:, j, :], ACT.Square).then_inc(lat_sq_ready, 1)
                g = l * 2 + (GAINS["mla_q_norm"] + j) if j < 2 else l + GAINS["mla_kv_norm"]
                sc.activation(lat_hi[:, j, :], lat[:, j, :], ACT.Copy,
                              scale=gain[:, bass.ds(g, 1)]).then_inc(lat_hi_ready, 1)

            sc.preload_act_table_set(EXP_LN)
            sc.wait_ge(gain_ready, 1)
            for d in range(KD):
                x_tile(0, d, slice(d, d + 1))
                for p in FIRST_SPLITS.get(d, []):
                    split_hi(0, 0, p)
            sc.dma_start(causal[:], a["c_tables"][0]).then_inc(consts_in, 16)
            sc.dma_start(sel_col[:], a["c_sel"]).then_inc(consts_in, 16)
            with nc.allow_non_contiguous_dma(reason="eight numbers"):
                sc.dma_start(fbias[2 * ROPE:2 * ROPE + G, :],
                             a["forget_bias"].rearrange("l g -> g l")).then_inc(consts_in, 16)
            with sc.Fori(0, DEPTH) as l:
                ffn(l, 0, 0, N_FFN1)
                table_in(1, 0)
                table_in(2, 1)
                for p in range(4):
                    split_hi(l, MIX0 + 1, p)
                    if p == 0:
                        norm_guess(l, N_MIX)
                    if p < 3:
                        latent(l, p)
                sc.wait_ge(rope_done, l * 5 + 1)
                sc.activation(k1[HD:HD + ROPE, 1:G, :],
                              k1[HD:HD + ROPE, 0:1, :].to_broadcast([ROPE, G - 1, T]), ACT.Copy
                              ).then_inc(rope_keys, 1)
                latent_guesses(l)
                split_hi(l, MIX0 + 2, 0)
                queries_keys_hi(l, 1, 0)
                split_hi(l, MIX0 + 2, 1)
                queries_keys_hi(l, 1, 1)
                split_hi(l, MIX0 + 2, 2)
                split_hi(l, MIX0 + 2, 3)
                split_hi(l, MIX0 + 3, 0)
                queries_keys_hi(l, 2, 0)
                for n in range(HEADS + 1):
                    if n < HEADS:
                        for i in range(QT):
                            if i == 0:
                                for m, p in operands_in(n):
                                    queries_keys_hi(l, m, p)
                            if i == 2:
                                for m, p in freed_panels(n):
                                    split_hi(l, MIX0 + m + 1, p)
                            if n not in SCORED and i == QT - 1:
                                copy_pt(l, n - 1)
                            sc.wait_ge(logits_ready, l * (4 * HEADS) + 4 * n + i + 1)
                            pr = prob[n % 2][:, TRI[i]:TRI[i + 1]]
                            sc.activation(pr, pr, ACT.Exp, scale=-1.0, bias=neg_max[:, n % 2, i:i + 1],
                                          accum_out=row_sum[:, n % 4, i:i + 1]).then_inc(exp_ready, 1)
                        if ORDER[min(n + 2, HEADS - 1) // G] in "AD" and n + 2 < HEADS:
                            mixer, h = head_out(n + 2)
                            table_in((3 if mixer == "A" else 7) + h, n % 2)
                    if (n, 0) in SLOT_OT:
                        outputs_hi(l, SLOT_OT[n, 0], 0)
                    if n in SCORED and n or n == HEADS:
                        copy_pt(l, n - 1)
                    if n == 1:
                        sc.wait_ge(gate_step, l * 9 + 2)
                        g_ = gate[0:G, :]
                        sc.activation(g_, g_, ACT.Exp).then_inc(gate_exp, 1)
                        sc.wait_ge(gate_exp, l * 2 + 1)
                        sc.activation(g_, g_, ACT.Ln, bias=ones[0:G, 0:1]).then_inc(gate_exp, 1)
                    if (n, 1) in SLOT_OT:
                        outputs_hi(l, SLOT_OT[n, 1], 1)
                outputs_hi(l, "D", 0)
                outputs_hi(l, "D", 1, bank[2])
                for m in (6, 7):
                    for p in range(4):
                        split_hi(l, MIX0 + m + 1, p)
                        d = 4 * (m - 6) + p
                        x_tile(l * 3 + 2, d, gain_at(l, 2, d))
                ffn(l, FFN2, 2, N_FFN2)
            sc.preload_act_table_set(EXP_LN)
            sc.wait_ge(small_free, DEPTH * LAYER_USES + 1)
            sc.activation(inv_sum[:, 1, :], inv_sum[:, 0, :], ACT.Ln).then_inc(ln_done, 1)
            sc.wait_ge(ln_done, DEPTH * NORMS + 1)
            sc.activation(inv_sum[:, 1, :], inv_sum[:, 1, :], ACT.Exp, scale=-0.5).then_inc(guess, 1)
            sc.wait_ge(rs_ready, DEPTH * NORMS + 1)
            for q in range(QT):
                sc.wait_ge(turned, KD + q + 1)
                sc.activation(y_rows[:, q, 0:D // 2], bank[2 * q][:], ACT.Copy, scale=neg_max[:, 1, q:q + 1]
                              ).then_inc(y_even, 1)

        @block.gpsimd
        def _(po):
            def add_squares(m):
                for d in range(1, KD):
                    po.wait_ge(sq_ready, m * KD + d + 1)
                    if d > 1:
                        po.wait_ge(sq_summed, m * (KD - 1) + d - 1)
                    po.tensor_tensor(act[0][:], act[0][:], tmp[d % 2][:], ALU.add).then_inc(sq_summed, 1)

            def ffn(l, second, nth, nrm):
                with po.Fori(0, GU_STEPS) as i:
                    for j in range(2):
                        po.wait_ge(rs_ready, l * NORMS + nrm + 1)
                        po.wait_ge(silu_ready, l * (2 * KF) + (KF if second else 0) + i * 2 + j + 1)
                        po.tensor_tensor(tmp[j][:], tmp[j][:], rs[:], ALU.mult).then_inc(silu_scaled, 1)
                add_squares(l * 3 + nth + 1)

            add_squares(0)
            with po.Fori(0, DEPTH) as l:
                ffn(l, False, 0, N_FFN1)
                po.wait_ge(lat_sq_ready, l * 3 + 2)
                po.tensor_tensor(lat_sq[:, 0, :], lat_sq[:, 0, :], lat_sq[:, 1, :], ALU.add).then_inc(lat_summed, 1)
                for j in range(2):
                    po.wait_ge(out_free, l * MIX_OUTS + mix_out(1, 2, 2 + j) + 1)
                    po.wait_ge(tab_in[j], l * 80 + 16)
                    po.tensor_tensor(rot[:, j, :], rot[:, j, :], tab[j][:], ALU.mult).then_inc(rope_mul, 1)
                add_squares(l * 3 + 2)
                ffn(l, True, 2, N_FFN2)

        @block.vector
        def _(dv):
            def split_lo(l, s, p, step=None):
                step = s if step is None else step
                dv.wait_ge(hi_ready, l * (4 * LAYER_STEPS) + step * 4 + p + 1)
                for how, src in pieces(s, p):
                    for (d, v), (h_, _) in zip(each_piece(how, lambda q: place(lo[p], q), src),
                                               each_piece(how, lambda q: place(hi[p], q), src)):
                        last = dv.tensor_tensor(d, v, h_.bitcast(F32), ALU.subtract)
                last.then_inc(lo_ready, 1)

            def x_lo(nth, d, g):
                dv.wait_ge(xg_hi_ready, nth + 1)
                dv.scalar_tensor_tensor(xg_lo[:, d, :], x[:, d, :], gain[:, g], xg_hi[:, d, :].bitcast(F32),
                                        ALU.mult, ALU.subtract).then_inc(xg_lo_ready, 1)

            def x_tile(l, src, nth, d, g, half):
                dv.scalar_tensor_tensor(x[:, d, :], src[:], half, x[:, d, :], ALU.mult, ALU.add
                                        ).then_inc(x_ready, 1)
                x_lo(nth, d, g)

            def gain_at(l, g, d):
                return gain_col(l, g, d)

            def mean_square(l, n, width, src, v):
                use = (U_FFN1, U_MIX, U_LQ, U_LKV, U_FFN2)[n]
                dv.wait_ge(small_full, l * LAYER_USES + use + 1)
                dv.tensor_scalar(v, src[:], 1.0 / width, EPS, ALU.mult, ALU.add).then_inc(small_free, 1)

            def refine(l, n, v, r, dst, t=act[1][:]):
                c = l * NORMS + n
                dv.wait_ge(guess, c + 1)
                dv.tensor_tensor(t, r, r, ALU.mult).then_inc(newton, 1)
                dv.wait_ge(newton, c * 2 + 1)
                dv.scalar_tensor_tensor(t, t, -0.5, v, ALU.mult, ALU.mult).then_inc(newton, 1)
                dv.wait_ge(newton, c * 2 + 2)
                dv.scalar_tensor_tensor(dst, t, 1.5, r, ALU.add, ALU.mult).then_inc(rs_ready, 1)
                dv.wait_ge(rs_ready, c + 1)

            def norm(l, n, width, dst):
                mean_square(l, n, width, SMALL, tmp[0][:])
                refine(l, n, tmp[0][:], tmp[1][:], dst)

            def panel_done(l, step, p):
                dv.wait_ge(panel_used, l * (4 * LAYER_STEPS) + step * 4 + p + 5)

            def ffn(l, s0, nth, nrm):
                def gate_up(i, following, step, first=False):
                    for p in range(4):
                        if first and p == 0:
                            norm(l, nrm, D, rs[:])
                        j, f = p % 2, l * (2 * KF) + (KF if s0 else 0) + i * 2 + p % 2 + 1
                        panel_done(l, s0 + i, p)
                        if p < 2:
                            dv.tensor_tensor(tmp[j][:], bank[p][:], rs[:], ALU.mult).then_inc(gated, 1)
                        else:
                            dv.wait_ge(silu_scaled, f)
                            dv.tensor_tensor(act[j][:], bank[p][:], tmp[j][:], ALU.mult).then_inc(a_ready, 1)
                        split_lo(l, following, p, step)
                        if p >= 2:
                            dv.wait_ge(a_hi_ready, f)
                            dv.tensor_tensor(a_lo[:, bass.ds(i * 2 + j, 1), :], act[j][:].unsqueeze(1),
                                             a_hi[:, bass.ds(i * 2 + j, 1), :].bitcast(F32),
                                             ALU.subtract).then_inc(a_lo_ready, 1)

                gate_up(0, s0, s0 + 1, first=True)
                with dv.Fori(1, GU_STEPS - 1) as i:
                    gate_up(i, s0, s0 + i + 1)
                gate_up(GU_STEPS - 1, s0 + GU_STEPS, s0 + GU_STEPS)
                for b in range(3 * DN_PAIRS):
                    s = s0 + GU_STEPS + b // 2
                    for h in range(2):
                        p = 2 * (b % 2) + h
                        if b % 3 == 2:
                            panel_done(l, s, p)
                            d = 2 * (b // 3) + h
                            x_tile(l, bank[4 + h], l * LAYER_X + KD * (nth + 1) + d, d, gain_at(l, nth + 1, d), 0.5)
                        split_lo(l, s + 1, p)

            def emptied(l, o, dst, src, by):
                dv.tensor_tensor(dst, src, by, ALU.mult).then_inc(out_free, 1)

            def values_turned(l, mixer, pair):
                dv.wait_ge(small_full, l * LAYER_USES + U_VT[mixer] + pair + 1)
                dv.tensor_copy(values[mixer][:, :, P * pair:P * (pair + 1)],
                               SMALL[:].rearrange("p (q c) -> p q c", q=QT)).then_inc(small_free, 1)

            def outputs_lo(l, mixer, pair, src=SMALL):
                dv.wait_ge(mix_hi_ready, l * KD + 2 * ORDER.index(mixer) + pair + 1)
                row = ROWS[mixer] + pair
                dv.tensor_tensor(mix_lo[:, row, :], src[:], mix_hi[:, row, :].bitcast(F32), ALU.subtract
                                 ).then_inc(small_free, 1)

            def turned_in_slot(l, n, pair):
                if (n, pair) in SLOT_VT:
                    values_turned(l, SLOT_VT[n, pair], pair)
                if (n, pair) in SLOT_OT:
                    outputs_lo(l, SLOT_OT[n, pair], pair)

            def latents_and_rotary_key(l):
                for p in range(4):
                    if p == 0:
                        norm(l, N_MIX, D, rs[:])
                    panel_done(l, MIX0, p)
                    if p < 3:
                        emptied(l, p, lat[:, p, :], bank[p][:], rs[:])
                        split_lo(l, MIX0 + 1, p)
                        dv.wait_ge(lat_hi_ready, l * 3 + p + 1)
                        g = l * 2 + (GAINS["mla_q_norm"] + p) if p < 2 else l + GAINS["mla_kv_norm"]
                        dv.scalar_tensor_tensor(lat_lo[:, p, :], lat[:, p, :], gain[:, bass.ds(g, 1)],
                                                lat_hi[:, p, :].bitcast(F32), ALU.mult, ALU.subtract
                                                ).then_inc(lat_lo_ready, 1)
                    else:
                        n = 2 * ROPE + G
                        emptied(l, p, k_misc[0:n, :], bank[p][0:n, :], rs[0:n, :])
                        split_lo(l, MIX0 + 1, p)
                        dv.wait_ge(out_free, l * MIX_OUTS + p + 1)
                        for j in range(2):
                            dv.wait_ge(tab_in[j], l * 80 + 16)
                        dv.tensor_tensor(k_rot[0:ROPE, :], k_misc[0:ROPE, :], tab[0][0:ROPE, :], ALU.mult
                                         ).then_inc(rope_in, 1)
                        dv.tensor_tensor(gate[0:ROPE, :], k_misc[ROPE:2 * ROPE, :], tab[1][ROPE:2 * ROPE, :], ALU.mult
                                         ).then_inc(rope_in, 1)
                        dv.wait_ge(rope_in, l * 2 + 2)
                        dv.tensor_tensor(k1[HD:HD + ROPE, 0, :], k_rot[0:ROPE, :], gate[0:ROPE, :], ALU.add
                                         ).then_inc(rope_done, 1)

            def up_projections(l):
                for p in (2, 3):
                    by, dst = lat_rs[:, p - 2, :], (q1, k1)[p - 2]
                    for o in range(4):
                        j = mix_out(1, p, o)
                        src = bank[out_bank(j)[0]]
                        if o < 3:
                            dv.wait_ge(up_full, l * 6 + 3 * (p - 2) + o + 1)
                        else:
                            panel_done(l, MIX0 + 1, p)
                        if o < 2:
                            dv.tensor_tensor(dst[0:HD, 2 * o, :], src[0:HD, :], by[0:HD, :], ALU.mult)
                            emptied(l, j, dst[0:HD, 2 * o + 1, :], src[HD:P, :], by[HD:P, :])
                        elif p == 2:
                            emptied(l, j, rot[:, o - 2, :], src[:], by)
                        else:
                            emptied(l, j, tmp[o - 2][:], src[:], by)
                    if p == 2:
                        split_lo(l, MIX0 + 2, p)
                dv.wait_ge(rope_mul, l * 2 + 2)
                for h in range(G):
                    r = slice(ROPE * h, ROPE * (h + 1))
                    dv.tensor_tensor(q1[HD:HD + ROPE, h, :], rot[r, 0, :], rot[r, 1, :], ALU.add).then_inc(rope_done, 1)
                split_lo(l, MIX0 + 2, 3)

            def project(l, m, p):
                panel_done(l, MIX0 + m, p)
                name = DEST[m, p]
                pair = int(name[2])
                if split_operand(m, p) is not None:
                    if split_operand(m, p) >= 2:
                        dv.wait_ge(operand_lo, l * (6 * G) + 2 * split_operand(m, p) - 2)
                dst = act[pair][:] if name[0] != "v" else tmp[pair][:]
                emptied(l, mix_out(m, p), dst, bank[out_bank(mix_out(m, p))[0]][:], rs[:])

            def queries_keys_lo(l, m, p):
                kind, mixer, pair = DEST[m, p][0], DEST[m, p][1], int(DEST[m, p][2])
                dv.wait_ge(operand_hi, l * (6 * G // 2) + split_operand(m, p) + 1)
                for e in range(2):
                    own, other = slice(HD * e, HD * (e + 1)), slice(HD * (1 - e), HD * (2 - e))
                    h = 2 * pair + e
                    if kind == "q":
                        dv.tensor_tensor(split_q[mixer][other, h, :], act[pair][own, :],
                                         split_q[mixer][own, h, :].bitcast(F32), ALU.subtract).then_inc(operand_lo, 1)
                    else:
                        dv.tensor_tensor(keys_lo[mixer][own, pair, :], act[pair][own, :],
                                         keys_hi[mixer][pair][own, e, :].bitcast(F32), ALU.subtract).then_inc(operand_lo, 1)

            def gates(l, n):
                z, g_ = gate_z, gate[0:G, :]
                if n == 1:
                    dv.tensor_scalar(z, k_misc[2 * ROPE:2 * ROPE + G, :],
                                     fbias[2 * ROPE:2 * ROPE + G, bass.ds(l, 1)], None, ALU.add
                                     ).then_inc(gate_step, 1)
                    dv.wait_ge(gate_step, l * 9 + 1)
                    dv.scalar_tensor_tensor(g_, z, -1.0, z, ALU.mult, ALU.min).then_inc(gate_step, 1)
                elif n == 2:
                    dv.wait_ge(gate_exp, l * 2 + 2)
                    dv.scalar_tensor_tensor(z, z, 0.0, g_, ALU.min, ALU.subtract).then_inc(gate_step, 1)
                elif n == 3:
                    dv.wait_ge(gate_step, l * 9 + 3)
                    dv.tensor_tensor_scan(g_, ones[0:G, 0:1].to_broadcast([G, T]), z, 0.0, ALU.mult, ALU.add
                                          ).then_inc(gate_step, 1)
                elif n == 4:
                    dv.wait_ge(gate_step, l * 9 + 4)
                    dv.tensor_scalar(z, g_, -1.0 / SCALE, None, ALU.mult).then_inc(gate_step, 1)
                elif n == 5:
                    dv.wait_ge(gate_step, l * 9 + 5)
                    dv.tensor_copy(dec[0:G, :], z).then_inc(gate_step, 1)
                    dv.tensor_copy(dec[64:64 + G, :], z).then_inc(gate_step, 1)
                elif n == 6:
                    dv.wait_ge(gate_step, l * 9 + 6)
                    for r in (32, 96):
                        dv.tensor_tensor(dec[r:r + G, :], z, dec[0:G, :].bitcast(F32), ALU.subtract
                                         ).then_inc(gate_step, 1)
                elif n == 3 * G:
                    dv.tensor_copy(ident_r, ident[:]).then_inc(ident_ready, 1)

            def refill(l, n):
                for m, p in freed_panels(n):
                    split_lo(l, MIX0 + m + 1, p)

            def logits(l, n, i):
                mixer, h = head_out(n)
                table, scale = causal, SCALE_MLA if mixer == "C" else SCALE
                if mixer in "AD":
                    table = tab[n % 2]
                dv.wait_ge(s_full, 4 * n + i + 1)
                w = P * (i + 1)
                dv.tensor_tensor_reduce(prob[n % 2][:, TRI[i]:TRI[i + 1]], bank[S_BANK[i % 2]][:, 0:w],
                                        table[:, T - w:T], -scale, BIG, ALU.add, ALU.min,
                                        neg_max[:, n % 2, i:i + 1]).then_inc(logits_ready, 1)

            def copy_pt(l, n, kt):
                dv.wait_ge(pt_full, l * (3 * HEADS) + 3 * n + (3 if kt else 1))
                if n >= 2:
                    dv.wait_ge(o_full, l * HEADS + n - 1)
                w = T - P * kt
                dv.tensor_copy(probT[n % 2][:, TRT[kt]:TRT[kt] + w], PT_EVEN[:, P * kt:T]).then_inc(pt_even, 1)

            def outputs(l, n):
                _, h = head_out(n)
                dv.wait_ge(o_full, l * HEADS + n + 1)
                dv.reciprocal(inv_sum[:, n % 2, :], row_sum[:, n % 4, :]).then_inc(inv_ready, 1)
                dv.wait_ge(inv_ready, l * HEADS + n + 1)
                dv.tensor_tensor(o_rows[:, :, HD * h:HD * (h + 1)],
                                 O_BANK[:, 0:QT * HD].rearrange("p (q c) -> p q c", q=QT),
                                 inv_sum[:, n % 2, :].unsqueeze(2).to_broadcast([P, QT, HD]),
                                 ALU.mult).then_inc(o_ready, 1)

            dv.memset(ones[:], 1.0).then_inc(setup_done, 1)
            dv.memset(dec[:].bitcast(F32), 0.0).then_inc(setup_done, 1)
            dv.memset(sel[:].bitcast(F32), 0.0).then_inc(setup_done, 1)
            dv.memset(inv_sum[:], 0.0).then_inc(panel_used, 4)
            dv.memset(neg_max[:], 0.0).then_inc(lo_ready, 4)
            dv.memset(row_sum[:], 0.0).then_inc(setup_done, 1)
            dv.wait_ge(gain_full, 1)
            dv.tensor_copy(gain[:], SMALL[:, 0:GAIN_ROWS]).then_inc(gain_ready, 1)
            dv.wait_ge(gain_ready, 1)
            for d in range(KD + 1):
                if d < KD:
                    dv.wait_ge(turned, d + 1)
                    dv.tensor_copy(x[:, d, :], bank[X_BANKS[d % len(X_BANKS)]][:]).then_inc(x_ready, 1)
                if d:
                    dv.wait_ge(x_ready, d)
                    x_lo(d - 1, d - 1, slice(d - 1, d))
                    for p in FIRST_SPLITS.get(d - 1, []):
                        split_lo(0, 0, p)
            dv.wait_ge(consts_in, 16 * 3)
            dv.wait_ge(setup_done, 4)
            for r in range(0, P, 32):
                dv.tensor_copy(sel[r:r + G, :, :], sel_col[r:r + G, :].unsqueeze(2).to_broadcast([G, G, P])
                               ).then_inc(setup_done, 1)
            with dv.Fori(0, DEPTH) as l:
                ffn(l, 0, 0, N_FFN1)
                latents_and_rotary_key(l)
                mean_square(l, N_LQ, Q_RANK, SMALL, LAT_V[0])
                mean_square(l, N_LKV, KV_RANK, LKV_BANK, LAT_V[1])
                project(l, 1, 0)
                for j, n in enumerate((N_LQ, N_LKV)):
                    refine(l, n, LAT_V[j], LAT_GUESS[j], lat_rs[:, j, :])
                split_lo(l, MIX0 + 2, 0)
                project(l, 1, 1)
                split_lo(l, MIX0 + 2, 1)
                up_projections(l)
                queries_keys_lo(l, 1, 0)
                project(l, 2, 0)
                split_lo(l, MIX0 + 3, 0)
                for n in range(HEADS + 1):
                    if n < HEADS:
                        for i in range(QT):
                            if i == QT - 1 and n in SCORED:
                                project(l, *SCORED[n])
                            if i == 2 and n not in SCORED:
                                copy_pt(l, n - 1, 0)
                            if i == 2:
                                if n == 0:
                                    queries_keys_lo(l, 1, 1)
                                    queries_keys_lo(l, 2, 0)
                                for m, p in operands_in(n):
                                    queries_keys_lo(l, m, p)
                                if n not in LATE_SPLITS:
                                    refill(l, n)
                            logits(l, n, i)
                    turned_in_slot(l, n, 0)
                    if n in SCORED and n or n == HEADS:
                        copy_pt(l, n - 1, 0)
                    if n >= 2:
                        outputs(l, n - 2)
                    if n + 1 < HEADS and ORDER[(n + 1) // G] in "AD":
                        mixer, h = head_out(n + 1)
                        earlier = 1 + h // 2 + (2 if mixer == "D" else 0)
                        dv.wait_ge(tab_in[(n + 1) % 2], l * 80 + 16 * (earlier + 1))
                    if n:
                        copy_pt(l, n - 1, 2)
                    if n in LATE_SPLITS:
                        refill(l, n)
                    gates(l, n)
                    turned_in_slot(l, n, 1)
                    if n in LATER:
                        project(l, *LATER[n])
                outputs(l, HEADS - 1)
                outputs_lo(l, "D", 0)
                outputs_lo(l, "D", 1, bank[2])
                dv.sem_clear(s_full)
                for m in (6, 7):
                    for p in range(4):
                        panel_done(l, MIX0 + m, p)
                        d = 4 * (m - 6) + p
                        x_tile(l, bank[WO_BANK[p]], l * LAYER_X + 2 * KD + d, d, gain_at(l, 2, d), 1.0)
                        split_lo(l, MIX0 + m + 1, p)
                ffn(l, FFN2, 2, N_FFN2)
            mean_square(DEPTH, N_FFN1, D, LAST_SUMS, inv_sum[:, 0, :])
            refine(DEPTH, N_FFN1, inv_sum[:, 0, :], inv_sum[:, 1, :], neg_max[:, 1, :], neg_max[:, 0, :])
            for q in range(QT):
                dv.wait_ge(turned, KD + q + 1)
                dv.tensor_scalar(y_rows[:, q, D // 2:D], bank[2 * q + 1][:], neg_max[:, 1, q:q + 1], None, ALU.mult
                                 ).then_inc(y_odd, 1)


def tables():
    t = np.arange(P)[:, None] + (T - P)
    dist = (t - np.arange(T)[None, :]).astype(np.int64)
    ok = dist >= 0
    f = np.float32
    out = [np.where(ok, 0.0, NEG)]
    inv = f(10000.0) ** (-np.arange(0, ROPE, 2, dtype=f) / f(ROPE))
    ang = inv[:, None] * np.arange(T, dtype=f)[None, :]
    cos, sin = np.cos(ang, dtype=f), np.sin(ang, dtype=f)
    out.append(np.tile(np.concatenate([cos, cos]), (G, 1)))
    out.append(np.tile(np.concatenate([-sin, sin]), (G, 1)))
    slopes = [2.0 ** (-8.0 * (i + 1) / (2 * G)) for i in range(2 * G)]
    count = (dist <= 128).astype(int) + (dist % 4 == 0) * (dist <= 512) + (dist % 16 == 0) * (dist <= 2048)
    log_count = np.log(np.maximum(count, 1).astype(np.float64))
    for s in slopes[1::2]:
        out.append(np.where(ok, -s * dist / SCALE, NEG))
    for s in slopes[0::2]:
        out.append(np.where(ok & (count > 0), (log_count - s * dist) / SCALE, NEG))
    return np.stack(out).astype(f)


_INS = ["x", "norm_ffn1", "ffn1_gate", "ffn1_up", "ffn1_down", "norm_mix", "w_in", "forget_bias", "mla_q_norm",
        "mla_kv_norm", "w_uq", "w_ukv", "w_out", "norm_ffn2", "ffn2_gate", "ffn2_up", "ffn2_down", "norm_final"]


def kernel(**inputs):
    import concourse.bacc as bacc
    from concourse.bass_utils import run_bass_kernel_spmd

    nc = bacc.Bacc("TRN2", target_bir_lowering=False, num_devices=1)
    sel_col = np.zeros((P, G), np.float32)
    for r in range(0, P, 32):
        sel_col[r:r + G] = np.eye(G)
    host = {n: np.ascontiguousarray(inputs[n]) for n in _INS}
    host |= {"c_ident": np.eye(P, dtype=np.float32), "c_sel": sel_col, "c_tables": tables()}
    args = {n: nc.dram_tensor(f"in_{n}", v.shape, F32, kind="ExternalInput").ap() for n, v in host.items()}
    out = nc.dram_tensor("out", (1, T, D), F32, kind="ExternalOutput").ap()
    build(nc, args, out)
    r = run_bass_kernel_spmd(nc, [{f"in_{n}": v for n, v in host.items()}], core_ids=[0])
    return r.results[0]["out"]
```
